# Optimizing a Trainium2 kernel written in Bass

```python
import math, functools
import jax, jax.numpy as jnp
from jax import lax
import numpy as np

D_MODEL = 1024
BATCH = 1
SEQ = 512
DEPTH = 1
DEC_BATCH = 8
DEC_SEQ = 4
PAST_LEN = 2048
PAGE_SIZE = 128

SSM_WIDTH = D_MODEL // 2
SSM_GROUP = 16
SSM_GROUPS = SSM_WIDTH // SSM_GROUP
SSM_STATE = 64
NSA_HEADS = 8
HEAD_DIM = 64
NSA_WIDTH = NSA_HEADS * HEAD_DIM
NSA_KV = 2
NSA_REP = NSA_HEADS // NSA_KV
KV_WIDTH = NSA_KV * HEAD_DIM
BLK = 64
N_SEL = 16
WINDOW = 512
Q_CHUNK = 64
ROT_DIM = HEAD_DIM // 4
ROPE_THETA = 500000.0
MEM_LEN = 256
X_HEADS = 4
X_HEAD_DIM = 128
X_WIDTH = X_HEADS * X_HEAD_DIM
D_FF = 4 * D_MODEL
N_IN = SSM_WIDTH + NSA_WIDTH + 6 * KV_WIDTH + 3 * NSA_HEADS + 2 * D_MODEL
EPS = 1e-6
NEG_INF = -1e30
FORCE_SCORE = 1e4
F32 = jnp.float32

kernel_name = 'hybrid_s5_nsa_decode_step'

def rmsnorm(x, g):
    xf = x.astype(F32)
    y = xf * lax.rsqrt(jnp.mean(xf * xf, axis=-1, keepdims=True) + EPS) * g.astype(F32)
    return y.astype(x.dtype)

def partial_rope(x, pos):
    half = ROT_DIM // 2
    freqs = ROPE_THETA ** (-jnp.arange(half, dtype=F32) / half)
    ang = pos.astype(F32)[:, None] * freqs[None, :]
    cos = jnp.cos(ang)[:, None, :]
    sin = jnp.sin(ang)[:, None, :]
    xf = x.astype(F32)
    x1, x2 = xf[..., :half], xf[..., half:ROT_DIM]
    out = jnp.concatenate([x1 * cos - x2 * sin, x2 * cos + x1 * sin, xf[..., ROT_DIM:]], axis=-1)
    return out.astype(x.dtype)

def masked_softmax(s, mask, axis=-1):
    s = jnp.where(mask, s, NEG_INF)
    m = jnp.max(s, axis=axis, keepdims=True)
    p = jnp.exp(s - m) * mask
    return p / jnp.maximum(jnp.sum(p, axis=axis, keepdims=True), 1e-30)

def _linear_combine(left, right):
    a1, b1 = left
    a2, b2 = right
    return a1 * a2, a2 * b1 + b2

def ssm_branch(u, h0, p):
    bsz, t = u.shape[:2]
    uf = u.astype(F32)
    lam = lax.complex(p['ssm_lam_re'].astype(F32), p['ssm_lam_im'].astype(F32))
    dt = jnp.exp(p['ssm_log_dt'].astype(F32))[:, None]
    lam_bar = jnp.exp(lam * dt)
    b = lax.complex(p['ssm_b_re'].astype(F32), p['ssm_b_im'].astype(F32))
    b_bar = ((lam_bar - 1.0) / lam)[..., None] * b
    c = lax.complex(p['ssm_c_re'].astype(F32), p['ssm_c_im'].astype(F32))
    ug = uf.reshape(bsz, t, SSM_GROUPS, SSM_GROUP).astype(jnp.complex64)
    bu = jnp.einsum('gpc,btgc->btgp', b_bar, ug)
    a = jnp.broadcast_to(lam_bar, bu.shape)
    a_cum, b_cum = lax.associative_scan(_linear_combine, (a, bu), axis=1)
    h = a_cum * h0[:, None] + b_cum
    y = jnp.real(jnp.einsum('gcp,btgp->btgc', c, h)).reshape(bsz, t, SSM_WIDTH) + p['ssm_d'].astype(F32) * uf
    y = jax.nn.gelu(y)
    out = y * jax.nn.sigmoid(y @ p['w_glu'].astype(F32) + p['b_glu'].astype(F32))
    return out.astype(u.dtype), h[:, -1]

def nsa_compress(rows, pe, w1, w2):
    bsz, tk = rows.shape[:2]
    nb = tk // BLK
    blocks = rows.astype(F32).reshape(bsz, nb, BLK, NSA_KV, HEAD_DIM) + pe.astype(F32)[None, None, :, None, :]
    flat = blocks.transpose(0, 1, 3, 2, 4).reshape(bsz, nb, NSA_KV, BLK * HEAD_DIM)
    return jax.nn.gelu(flat @ w1.astype(F32)) @ w2.astype(F32)

def nsa_core(q, gates, q_pos, kcmp, vcmp, ks_t, vs_t, wk, wv, w_pos):
    bsz, tq = q.shape[:2]
    nb = kcmp.shape[1]
    qg = q.astype(F32).reshape(bsz, tq, NSA_KV, NSA_REP, HEAD_DIM) * (HEAD_DIM ** -0.5)
    blk_ids = jnp.arange(nb, dtype=jnp.int32)
    s_c = jnp.einsum('bqgrd,bngd->bqgrn', qg, kcmp)
    c_valid = ((blk_ids[None, :] + 1) * BLK - 1 <= q_pos[:, None])[None, :, None, None, :]
    p_c = masked_softmax(s_c, c_valid)
    o_c = jnp.einsum('bqgrn,bngd->bqgrd', p_c, vcmp)
    cur = q_pos // BLK
    jb = blk_ids[None, :]
    cq = cur[:, None]
    forced = ((jb == 0) | (jb == cq) | (jb == cq - 1))[None, :, None, :]
    allowed = (jb <= cq)[None, :, None, :]
    imp = jnp.where(forced, FORCE_SCORE, jnp.sum(p_c, axis=3))
    imp = jnp.where(allowed, imp, -FORCE_SCORE)
    k_sel = min(N_SEL, nb)
    _, idx = lax.top_k(imp, k_sel)
    b_ix = jnp.arange(bsz)[:, None, None, None]
    g_ix = jnp.arange(NSA_KV)[None, None, :, None]
    ks_g = ks_t[b_ix, g_ix, idx].astype(F32)
    vs_g = vs_t[b_ix, g_ix, idx].astype(F32).reshape(bsz, tq, NSA_KV, k_sel * BLK, HEAD_DIM)
    key_pos = idx[..., None] * BLK + jnp.arange(BLK, dtype=jnp.int32)
    s_mask = (key_pos <= q_pos[None, :, None, None, None]).reshape(bsz, tq, NSA_KV, 1, k_sel * BLK)
    s_s = jnp.einsum('bqgrd,bqgksd->bqgrks', qg, ks_g).reshape(bsz, tq, NSA_KV, NSA_REP, k_sel * BLK)
    p_s = masked_softmax(s_s, s_mask)
    o_s = jnp.einsum('bqgrn,bqgnd->bqgrd', p_s, vs_g)
    s_w = jnp.einsum('bqgrd,bngd->bqgrn', qg, wk.astype(F32))
    dpos = q_pos[:, None] - w_pos[None, :]
    w_valid = ((dpos >= 0) & (dpos < WINDOW) & (w_pos[None, :] >= 0))[None, :, None, None, :]
    p_w = masked_softmax(s_w, w_valid)
    o_w = jnp.einsum('bqgrn,bngd->bqgrd', p_w, wv.astype(F32))
    g = jax.nn.sigmoid(gates.astype(F32)).reshape(bsz, tq, NSA_KV, NSA_REP, 3)
    o = g[..., 0:1] * o_c + g[..., 1:2] * o_s + g[..., 2:3] * o_w
    return o.reshape(bsz, tq, NSA_WIDTH).astype(q.dtype)

def nsa_prompt(q, gates, k_cmp, v_cmp, k_sel, v_sel, k_win, v_win, p):
    bsz, t = q.shape[:2]
    nb = t // BLK
    kcmp = nsa_compress(k_cmp, p['cmp_pe_k'], p['w_cmpk1'], p['w_cmpk2'])
    vcmp = nsa_compress(v_cmp, p['cmp_pe_v'], p['w_cmpv1'], p['w_cmpv2'])
    ks_t = k_sel.reshape(bsz, nb, BLK, NSA_KV, HEAD_DIM).transpose(0, 3, 1, 2, 4)
    vs_t = v_sel.reshape(bsz, nb, BLK, NSA_KV, HEAD_DIM).transpose(0, 3, 1, 2, 4)
    wk_pad = jnp.pad(k_win, ((0, 0), (WINDOW, 0), (0, 0), (0, 0)))
    wv_pad = jnp.pad(v_win, ((0, 0), (WINDOW, 0), (0, 0), (0, 0)))
    n_chunks = t // Q_CHUNK
    q_c = q.reshape(bsz, n_chunks, Q_CHUNK, NSA_HEADS, HEAD_DIM).swapaxes(0, 1)
    g_c = gates.reshape(bsz, n_chunks, Q_CHUNK, 3 * NSA_HEADS).swapaxes(0, 1)

    def chunk(args):
        ci, qi, gi = args
        q0 = ci * Q_CHUNK
        q_pos = q0 + jnp.arange(Q_CHUNK, dtype=jnp.int32)
        w_pos = q0 - WINDOW + jnp.arange(WINDOW + Q_CHUNK, dtype=jnp.int32)
        wk_i = lax.dynamic_slice_in_dim(wk_pad, q0, WINDOW + Q_CHUNK, axis=1)
        wv_i = lax.dynamic_slice_in_dim(wv_pad, q0, WINDOW + Q_CHUNK, axis=1)
        return nsa_core(qi, gi, q_pos, kcmp, vcmp, ks_t, vs_t, wk_i, wv_i, w_pos)

    out = lax.map(chunk, (jnp.arange(n_chunks, dtype=jnp.int32), q_c, g_c))
    out = out.swapaxes(0, 1).reshape(bsz, t, NSA_WIDTH)
    rows = jnp.stack([k_cmp, v_cmp, k_sel, v_sel], axis=2)
    w_keep = min(WINDOW, t)
    win = jnp.stack([k_win, v_win], axis=2)[:, t - w_keep:]
    return out, (rows, win)

def nsa_sample(q, gates, k_cmp, v_cmp, k_sel, v_sel, k_win, v_win, p, cache_kv, page_table, win_buf):
    bsz, t = q.shape[:2]
    past_len = page_table.shape[1] * PAGE_SIZE
    past = cache_kv[page_table].reshape(bsz, past_len, 4, NSA_KV, HEAD_DIM)
    rows = jnp.stack([k_cmp, v_cmp, k_sel, v_sel], axis=2)
    total = past_len + t
    pad = (-total) % BLK
    full = jnp.pad(jnp.concatenate([past, rows.astype(past.dtype)], axis=1),
                   ((0, 0), (0, pad), (0, 0), (0, 0), (0, 0)))
    nb = (total + pad) // BLK
    kcmp = nsa_compress(full[:, :, 0], p['cmp_pe_k'], p['w_cmpk1'], p['w_cmpk2'])
    vcmp = nsa_compress(full[:, :, 1], p['cmp_pe_v'], p['w_cmpv1'], p['w_cmpv2'])
    ks_t = full[:, :, 2].reshape(bsz, nb, BLK, NSA_KV, HEAD_DIM).transpose(0, 3, 1, 2, 4)
    vs_t = full[:, :, 3].reshape(bsz, nb, BLK, NSA_KV, HEAD_DIM).transpose(0, 3, 1, 2, 4)
    w_buf_len = win_buf.shape[1]
    win_full = jnp.concatenate([win_buf, jnp.stack([k_win, v_win], axis=2).astype(win_buf.dtype)], axis=1)
    w_pos = past_len - w_buf_len + jnp.arange(w_buf_len + t, dtype=jnp.int32)
    q_pos = past_len + jnp.arange(t, dtype=jnp.int32)
    out = nsa_core(q, gates, q_pos, kcmp, vcmp, ks_t, vs_t, win_full[:, :, 0], win_full[:, :, 1], w_pos)
    return out, (rows, win_full[:, t:])

def memory_kv(mem, g_mem, w_xk, w_xv):
    bsz, m_len, _ = mem.shape
    mn = rmsnorm(mem, g_mem)
    k = (mn @ w_xk).reshape(bsz, m_len, X_HEADS, X_HEAD_DIM)
    v = (mn @ w_xv).reshape(bsz, m_len, X_HEADS, X_HEAD_DIM)
    return jnp.stack([k, v], axis=2)

def cross_attention(c, mem_kv, w_xq, w_xo):
    bsz, t, _ = c.shape
    q = (c @ w_xq).reshape(bsz, t, X_HEADS, X_HEAD_DIM).astype(F32) * (X_HEAD_DIM ** -0.5)
    s = jnp.einsum('bthd,bmhd->bhtm', q, mem_kv[:, :, 0].astype(F32))
    pr = jax.nn.softmax(s, axis=-1)
    o = jnp.einsum('bhtm,bmhd->bthd', pr, mem_kv[:, :, 1].astype(F32))
    return o.reshape(bsz, t, X_WIDTH).astype(c.dtype) @ w_xo

def decoder_layer(x, pos, h0, attend_fn, mem_kv, p):
    bsz, t, _ = x.shape
    a = rmsnorm(x, p['g_mix_pre'])
    proj = a @ p['w_in']
    o1 = SSM_WIDTH
    o2 = o1 + NSA_WIDTH
    o3 = o2 + 6 * KV_WIDTH
    o4 = o3 + 3 * NSA_HEADS
    u = proj[..., :o1]
    q = partial_rope(proj[..., o1:o2].reshape(bsz, t, NSA_HEADS, HEAD_DIM), pos)
    kv6 = proj[..., o2:o3].reshape(bsz, t, 6, NSA_KV, HEAD_DIM)
    nsa_gates = proj[..., o3:o4]
    merge_logits = proj[..., o4:]
    k_cmp = partial_rope(kv6[:, :, 0], pos)
    v_cmp = kv6[:, :, 1]
    k_sel = partial_rope(kv6[:, :, 2], pos)
    v_sel = kv6[:, :, 3]
    k_win = partial_rope(kv6[:, :, 4], pos)
    v_win = kv6[:, :, 5]
    ssm_out, h_last = ssm_branch(u, h0, p)
    nsa_out, nsa_state = attend_fn(q, nsa_gates, k_cmp, v_cmp, k_sel, v_sel, k_win, v_win, p)
    gates = jax.nn.sigmoid(merge_logits.astype(F32)).reshape(bsz, t, 2, D_MODEL)
    merged = (gates[:, :, 0] * (ssm_out @ p['w_br_ssm']).astype(F32)
              + gates[:, :, 1] * (nsa_out @ p['w_br_nsa']).astype(F32))
    x = x + rmsnorm(merged.astype(x.dtype) @ p['w_out'], p['g_mix_post'])
    c = rmsnorm(x, p['g_x_pre'])
    x = x + rmsnorm(cross_attention(c, mem_kv, p['w_xq'], p['w_xo']), p['g_x_post'])
    m = rmsnorm(x, p['g_mlp_pre'])
    hid = jnp.square(jax.nn.relu(m @ p['w_up']))
    x = x + rmsnorm(hid @ p['w_down'], p['g_mlp_post'])
    return x, h_last, nsa_state

def setup_inputs(seed: int = 0) -> dict:
    keys = iter(jax.random.split(jax.random.key(seed), 64))

    def nrm(shape, scale=1.0):
        return jax.random.normal(next(keys), shape, F32) * scale

    def gain():
        return 1.0 + nrm((DEPTH, D_MODEL), 0.02)

    n_pages = PAST_LEN // PAGE_SIZE
    n_used = DEC_BATCH * n_pages
    n_pool = n_used + max(1, n_used // 4)
    w_buf = min(WINDOW, PAST_LEN)
    page_table = jax.random.permutation(next(keys), n_pool)[:n_used].reshape(DEC_BATCH, n_pages).astype(jnp.int32)
    inv2 = 2.0 ** -0.5
    return {
        'x_prompt': nrm((BATCH, SEQ, D_MODEL)),
        'x_sample': nrm((DEC_BATCH, DEC_SEQ, D_MODEL)),
        'cache_nsa_kv': nrm((DEPTH, n_pool, PAGE_SIZE, 4, NSA_KV, HEAD_DIM)),
        'cache_win_kv': nrm((DEPTH, DEC_BATCH, w_buf, 2, NSA_KV, HEAD_DIM)),
        'state_ssm': nrm((DEPTH, DEC_BATCH, SSM_GROUPS, SSM_STATE, 2), 0.1),
        'cache_mem_kv': nrm((DEPTH, DEC_BATCH, MEM_LEN, 2, X_HEADS, X_HEAD_DIM)),
        'page_table': page_table,
        'mem_prompt': nrm((BATCH, MEM_LEN, D_MODEL)),
        'g_mix_pre': gain(),
        'w_in': nrm((DEPTH, D_MODEL, N_IN), D_MODEL ** -0.5),
        'ssm_lam_re': -0.5 + nrm((DEPTH, SSM_GROUPS, SSM_STATE), 0.01),
        'ssm_lam_im': jnp.pi * jnp.arange(SSM_STATE, dtype=F32) + nrm((DEPTH, SSM_GROUPS, SSM_STATE), 0.01),
        'ssm_log_dt': jax.random.uniform(next(keys), (DEPTH, SSM_GROUPS), F32, math.log(1e-3), math.log(1e-1)),
        'ssm_b_re': nrm((DEPTH, SSM_GROUPS, SSM_STATE, SSM_GROUP), inv2 * SSM_GROUP ** -0.5),
        'ssm_b_im': nrm((DEPTH, SSM_GROUPS, SSM_STATE, SSM_GROUP), inv2 * SSM_GROUP ** -0.5),
        'ssm_c_re': nrm((DEPTH, SSM_GROUPS, SSM_GROUP, SSM_STATE), inv2 * SSM_STATE ** -0.5),
        'ssm_c_im': nrm((DEPTH, SSM_GROUPS, SSM_GROUP, SSM_STATE), inv2 * SSM_STATE ** -0.5),
        'ssm_d': nrm((DEPTH, SSM_WIDTH)),
        'w_glu': nrm((DEPTH, SSM_WIDTH, SSM_WIDTH), SSM_WIDTH ** -0.5),
        'b_glu': nrm((DEPTH, SSM_WIDTH), 0.01),
        'cmp_pe_k': nrm((DEPTH, BLK, HEAD_DIM), 0.02),
        'w_cmpk1': nrm((DEPTH, BLK * HEAD_DIM, HEAD_DIM), (BLK * HEAD_DIM) ** -0.5),
        'w_cmpk2': nrm((DEPTH, HEAD_DIM, HEAD_DIM), HEAD_DIM ** -0.5),
        'cmp_pe_v': nrm((DEPTH, BLK, HEAD_DIM), 0.02),
        'w_cmpv1': nrm((DEPTH, BLK * HEAD_DIM, HEAD_DIM), (BLK * HEAD_DIM) ** -0.5),
        'w_cmpv2': nrm((DEPTH, HEAD_DIM, HEAD_DIM), HEAD_DIM ** -0.5),
        'w_br_ssm': nrm((DEPTH, SSM_WIDTH, D_MODEL), SSM_WIDTH ** -0.5),
        'w_br_nsa': nrm((DEPTH, NSA_WIDTH, D_MODEL), NSA_WIDTH ** -0.5),
        'w_out': nrm((DEPTH, D_MODEL, D_MODEL), D_MODEL ** -0.5),
        'g_mix_post': gain(),
        'g_x_pre': gain(),
        'g_mem': gain(),
        'w_xq': nrm((DEPTH, D_MODEL, X_WIDTH), D_MODEL ** -0.5),
        'w_xk': nrm((DEPTH, D_MODEL, X_WIDTH), D_MODEL ** -0.5),
        'w_xv': nrm((DEPTH, D_MODEL, X_WIDTH), D_MODEL ** -0.5),
        'w_xo': nrm((DEPTH, X_WIDTH, D_MODEL), X_WIDTH ** -0.5),
        'g_x_post': gain(),
        'g_mlp_pre': gain(),
        'w_up': nrm((DEPTH, D_MODEL, D_FF), D_MODEL ** -0.5),
        'w_down': nrm((DEPTH, D_FF, D_MODEL), D_FF ** -0.5),
        'g_mlp_post': gain(),
    }

def reference(x_prompt, x_sample, cache_nsa_kv, cache_win_kv, state_ssm, cache_mem_kv, page_table, mem_prompt,
              g_mix_pre, w_in, ssm_lam_re, ssm_lam_im, ssm_log_dt, ssm_b_re, ssm_b_im, ssm_c_re, ssm_c_im,
              ssm_d, w_glu, b_glu, cmp_pe_k, w_cmpk1, w_cmpk2, cmp_pe_v, w_cmpv1, w_cmpv2,
              w_br_ssm, w_br_nsa, w_out, g_mix_post, g_x_pre, g_mem, w_xq, w_xk, w_xv, w_xo, g_x_post,
              g_mlp_pre, w_up, w_down, g_mlp_post):
    pos_p = jnp.arange(x_prompt.shape[1], dtype=jnp.int32)
    pos_s = PAST_LEN + jnp.arange(x_sample.shape[1], dtype=jnp.int32)
    y_p, y_s = x_prompt, x_sample
    kv_p, kv_s, win_p, win_s, ssm_p, ssm_s, mem_p = [], [], [], [], [], [], []
    for l in range(DEPTH):
        p = dict(g_mix_pre=g_mix_pre[l], w_in=w_in[l], ssm_lam_re=ssm_lam_re[l], ssm_lam_im=ssm_lam_im[l],
                 ssm_log_dt=ssm_log_dt[l], ssm_b_re=ssm_b_re[l], ssm_b_im=ssm_b_im[l], ssm_c_re=ssm_c_re[l],
                 ssm_c_im=ssm_c_im[l], ssm_d=ssm_d[l], w_glu=w_glu[l], b_glu=b_glu[l], cmp_pe_k=cmp_pe_k[l],
                 w_cmpk1=w_cmpk1[l], w_cmpk2=w_cmpk2[l], cmp_pe_v=cmp_pe_v[l], w_cmpv1=w_cmpv1[l],
                 w_cmpv2=w_cmpv2[l], w_br_ssm=w_br_ssm[l], w_br_nsa=w_br_nsa[l], w_out=w_out[l],
                 g_mix_post=g_mix_post[l], g_x_pre=g_x_pre[l], w_xq=w_xq[l], w_xo=w_xo[l],
                 g_x_post=g_x_post[l], g_mlp_pre=g_mlp_pre[l], w_up=w_up[l], w_down=w_down[l],
                 g_mlp_post=g_mlp_post[l])
        mem_kv_l = memory_kv(mem_prompt, g_mem[l], w_xk[l], w_xv[l])
        h0_p = jnp.zeros((x_prompt.shape[0], SSM_GROUPS, SSM_STATE), jnp.complex64)
        y_p, h_p, (rows_p, wst_p) = decoder_layer(y_p, pos_p, h0_p, nsa_prompt, mem_kv_l, p)
        h0_s = lax.complex(state_ssm[l, ..., 0].astype(F32), state_ssm[l, ..., 1].astype(F32))
        sample_fn = functools.partial(nsa_sample, cache_kv=cache_nsa_kv[l], page_table=page_table,
                                      win_buf=cache_win_kv[l])
        y_s, h_s, (rows_s, wst_s) = decoder_layer(y_s, pos_s, h0_s, sample_fn, cache_mem_kv[l], p)
        kv_p.append(rows_p)
        kv_s.append(rows_s)
        win_p.append(wst_p)
        win_s.append(wst_s)
        ssm_p.append(jnp.stack([jnp.real(h_p), jnp.imag(h_p)], axis=-1))
        ssm_s.append(jnp.stack([jnp.real(h_s), jnp.imag(h_s)], axis=-1))
        mem_p.append(mem_kv_l)
    kv_prompt = jnp.stack(kv_p)
    kv_sample = jnp.stack(kv_s)
    win_prompt = jnp.stack(win_p)
    win_sample = jnp.stack(win_s)
    ssm_prompt = jnp.stack(ssm_p)
    ssm_sample = jnp.stack(ssm_s)
    mem_kv_prompt = jnp.stack(mem_p)
    return (y_p, y_s, kv_prompt, kv_sample, win_prompt, win_sample, ssm_prompt, ssm_sample, mem_kv_prompt)


_drawn_inputs = setup_inputs


def setup_inputs(seed=0):
    import zlib

    import numpy as np

    out = dict(_drawn_inputs(seed))
    spreads = {}
    factors = {'g_mix_pre': 2.853,
     'ssm_lam_re': 62.288,
     'b_glu': 8.0,
     'cmp_pe_k': 7.227,
     'cmp_pe_v': 5.656,
     'g_mix_post': 4.011,
     'g_x_pre': 4.874,
     'g_mem': 2.89,
     'g_x_post': 15.198,
     'g_mlp_pre': 51.316,
     'g_mlp_post': 66.281}
    for name, (base, spread) in spreads.items():
        noise = np.random.default_rng([zlib.crc32(name.encode()), seed]).standard_normal(out[name].shape)
        drawn = base * np.exp(spread * noise) if base else spread * noise
        out[name] = __import__('jax').numpy.asarray(drawn.astype(out[name].dtype))
    for name, factor in factors.items():
        out[name] = (out[name] * factor).astype(out[name].dtype)
    return out
```

```python
import math
from contextlib import ExitStack

import numpy as np
import concourse.bass as bass
from concourse import mybir

F32 = mybir.dt.float32
I32 = mybir.dt.int32
ALU = mybir.AluOpType
ACT = mybir.ActivationFunctionType
AX = mybir.AxisListType

P = 128
D = 1024
KD = D // P
TP, DB, DQ = 512, 8, 4
TS = DB * DQ
TOK = TP + TS
HALF = TOK // 2
NT = 5
PAST, PAGE = 2048, 128
PAGES = PAST // PAGE
NPOOL = 160
G_SSM, C_SSM, S_SSM = 32, 16, 64
GP = G_SSM // 2
L = 8
NCH = TP // L
UROWS = NCH + 2 * DB
YROWS = NCH + DB
NH, HD, NKV, REP = 8, 64, 2, 4
BLK, NSEL = 64, 16
NBLK = PAST // BLK
WIN = 512
WT = WIN // P
MEM = 256
XH, XD = 4, 128
DFF = 4096
EPS = 1e-6
NEG = -1e30
TWO_PI = 2 * math.pi
ROUND = 12582912.0
GPG = 4 * PAGES
NG2 = 2

_C = {}
_w = 0
for _name, _n in (("ident", P), ("cos", NT * 8), ("sin", NT * 8), ("causal", P), ("cadd", 4 * 8), ("cmul", 4 * 8),
                  ("newadd", NG2 * TS), ("winadd", DQ), ("rows4", P), ("spread", NG2 * P), ("hmask", NH),
                  ("dmask", C_SSM), ("before", 900)):
    _C[_name] = (_w, _n)
    _w += _n
CW = _w


def constants():
    c = np.zeros((P, CW), np.float32)

    def put(name, a):
        o, n = _C[name]
        a = np.asarray(a, np.float32).reshape(len(a), n)
        c[:len(a), o:o + n] = a

    p = np.arange(P)
    put("ident", np.eye(P))
    pos = np.zeros((P, NT), np.float32)
    for t in range(4):
        pos[:, t] = t * P + p
    pos[:, 4] = PAST + p % DQ
    half = 8
    freqs = np.float32(500000.0) ** (-np.arange(half, dtype=np.float32) / np.float32(half))
    ang = pos[:, :, None] * freqs[None, None, :]
    put("cos", np.cos(ang))
    put("sin", np.sin(ang))
    put("causal", np.where(p[None, :] <= p[:, None], 0.0, NEG))
    q = np.arange(4)[None, :, None] * P + p[:, None, None]
    n = np.arange(8)[None, None, :]
    ok = (n + 1) * BLK - 1 <= q
    put("cadd", np.where(ok, 0.0, NEG))
    put("cmul", ok)
    b, g, i, r = p // 32, (p // 16) % 2, (p // 4) % 4, p % 4
    new = np.full((P, NG2, DB, DQ), NEG)
    for gg in range(NG2):
        for j in range(DQ):
            rows = p[j <= i]
            new[rows, gg, gg * 4 + b[rows], j] = 0.0
    put("newadd", new)
    put("winadd", np.where(np.arange(DQ)[None, :] > i[:, None], 0.0, NEG))
    put("rows4", (p[:, None] // 4) == (p[None, :] // 4))
    sp = np.zeros((TS, NG2, P))
    for gg in range(NG2):
        sp[(gg * 4 + b) * DQ + i, gg, p] = 1.0
    put("spread", sp)
    put("hmask", np.arange(NH)[None, :] == (g * REP + r)[:, None])
    put("dmask", (p[:, None] // C_SSM == L - 1) & (np.arange(C_SSM)[None, :] == p[:, None] % C_SSM))
    put("before", np.broadcast_to((np.arange(30)[None, :] < np.arange(30)[:, None]).reshape(1, 900), (P, 900)))
    return c


def hybrid_decoder_layer(nc, A, O):
    (y_prompt, y_sample, kv_prompt, kv_sample, win_prompt, win_sample, ssm_prompt, ssm_sample, mem_kv_prompt) = O
    us_dram = nc.dram_tensor("u_scratch", (TOK, 512), F32, kind="Internal").ap()
    gk_dram = nc.dram_tensor("toeplitz_scratch", (15 * C_SSM, 512), F32, kind="Internal").ap()

    ctx = ExitStack()
    with ctx:
        sems = {}

        def sem(name):
            if name not in sems:
                sems[name] = ctx.enter_context(nc.semaphore(name))
            return sems[name]

        ACOLS = 52900
        arena = ctx.enter_context(nc.sbuf_tensor("arena", [P, ACOLS], F32))
        page_ids = ctx.enter_context(nc.sbuf_tensor("page_ids", [1, DB * PAGES], I32))
        top = [0]

        def place(cols, at=None):
            if at is None:
                at = top[0]
                top[0] += cols
            assert at + cols <= ACOLS, (at, cols)
            return arena[:, at:at + cols]

        consts = place(CW)
        small = place(900)
        actT = place(KD * TOK).rearrange("p (k t) -> p k t", k=KD)
        RING = 3
        ring = place(RING * 2048).rearrange("p (s c) -> p s c", s=RING)
        att0 = top[0]
        kvt = place(NT * 768).rearrange("p (t c) -> p t c", t=NT)
        qT = place(REP * TOK).rearrange("p (r t) -> p r t", r=REP)
        kT = place(2 * TOK).rearrange("p (b t) -> p b t", b=2)
        gtk = place(NT * 24).rearrange("p (t c) -> p t c", t=NT)
        hz = place(2 * 2 * 68 * 2).rearrange("p (v g n h) -> p v g n h", v=2, g=2, n=68)
        kcT = place(272)
        vc = place(DB * P).rearrange("p (b c) -> p b c", b=DB)
        vcp = place(P)
        ssmT = place(4 * TOK).rearrange("p (k t) -> p k t", k=4)
        nsaT = place(4 * TOK).rearrange("p (k t) -> p k t", k=4)
        R = top[0]

        def C(name):
            o, n = _C[name]
            return consts[:, o:o + n]

        ident = C("ident")
        so = [0]

        def sm(n):
            so[0] += n
            assert so[0] <= 900
            return small[:, so[0] - n:so[0]]

        psum = ctx.enter_context(nc.psum_tensor("banks", [P, 8, 512], F32))

        def bank(b, cols=512, at=0, rows=P):
            return psum[0:rows, b, at:at + cols]

        x_a = place(NT * D, R + 12288).rearrange("p (t c) -> p t c", t=NT)
        xn = place(2 * D, R + 17408).rearrange("p (s c) -> p s c", s=2)
        junk = place(D, R + 20480)
        vecs = place(P, R + 7168)
        lamrow = place(2560, R + 4096).rearrange("p (v s) -> p v s", v=20)
        eps = sm(1)
        ssq = sm(16)
        rms = sm(16)
        rstd = sm(16)
        pv = sm(36)
        gain = {"mix": pv[:, 0:8], "x": pv[:, 8:16], "mlp": pv[:, 16:24], "mem": pv[:, 24:32]}
        bglu = pv[:, 32:36]
        fT = nsaT.rearrange("p k t -> p (k t)")[:, 0:2 * TOK].rearrange("p (s t) -> p s t", s=2)
        u_tok = place(NT * 512, R + 12288).rearrange("p (t c) -> p t c", t=NT)
        q_tok = place(NT * 512, R + 16384).rearrange("p (t c) -> p t c", t=NT)
        rope_t = place(2 * 320, R + 20480).rearrange("p (s c) -> p s c", s=2)

        BP = place(4096, R).rearrange("p (z g j c) -> p z g j c", z=2, g=GP, j=L)
        M1 = place(4096, R + 4096).rearrange("p (z g s) -> p z g s", z=2, g=GP)
        M2 = place(4096, R + 8192).rearrange("p (z g j c) -> p z g j c", z=2, g=GP, j=L)
        Tz = place(4096, R + 12288).rearrange("p (i c) -> p i c", i=L)
        U = place(4096, R + 16384).rearrange("p (j c) -> p j c", j=L)
        UT = place(G_SSM * UROWS, R + 20480).rearrange("p (g n) -> p g n", g=G_SSM)
        Z = place(2 * GP * UROWS, R + 23040).rearrange("p (z g n) -> p z g n", z=2, g=GP)
        bb = place(512, R + 23040).rearrange("p (z g c) -> p z g c", z=2, g=GP)
        b_in = place(512, R + 23552).rearrange("p (z g c) -> p z g c", z=2, g=GP)
        c_in = place(512, R + 24064).rearrange("p (z g c) -> p z g c", z=2, g=GP)
        cblk = place(1024, R + 24576).rearrange("p (z g m c) -> p z g m c", z=2, g=GP, m=2)
        c_raw = place(512, R + 24576).rearrange("p (z a s) -> p z a s", z=2, a=2)
        mtmp = place(512, R + 18944).rearrange("p (z g c) -> p z g c", z=2, g=GP)
        G = place(512, R + 21120)
        drow = place(512, R + 21632)
        dterm = place(512, R + 22144)
        zrow = place(512, R + 6656)
        E = place(2 * 1024, R).rearrange("p (z g n) -> p z g n", z=2, g=GP)
        rho = place(1024, R + 2048).rearrange("p (g n) -> p g n", g=GP)
        rt = place(1024, R + 3072).rearrange("p (g n) -> p g n", g=GP)
        W = place(2 * 1024, R + 4096).rearrange("p (z g n) -> p z g n", z=2, g=GP)
        Gs = place(2 * 1024, R + 6144).rearrange("p (z g n) -> p z g n", z=2, g=GP)
        U2 = [t.rearrange("p k t -> p (k t)")[:, 0:2048].rearrange("p (g j) -> p g j", g=16) for t in (ssmT, nsaT)]
        y_sb = U
        yg = place(4 * TOK, R).rearrange("p (k t) -> p k t", k=4)
        sg = place(4 * TOK, R + 2176).rearrange("p (k t) -> p k t", k=4)
        h0raw = sm(256)
        hfp = sm(2 * GP).rearrange("p (z g) -> p z g", z=2)
        hfs = sm(2 * DB * GP).rearrange("p (z b g) -> p z b g", z=2, b=DB)
        hout = place(512, R + 6656)
        lam_s = place(7 * GP, R + 25600).rearrange("p (v g) -> p v g", v=7)
        pw = place(2 * GP * 9, R + 25712).rearrange("p (z n g) -> p z n g", z=2, n=9)
        pwt = place(128, R + 26000)
        u8 = sm(32)
        cur = sm(64)
        assert R + 26128 <= ACOLS

        wc = place(8192, R + 4800).rearrange("p (d m) -> p d m", d=HD)
        cmp_units = [(v, s0, n) for v in range(2) for s0, n in ((0, 2), (2, 3), (5, 3))]
        CU = len(cmp_units)
        CN = 3 * PAGES
        NP0 = cmp_units[0][2] * PAGES
        ck = [place(CN * P, R + (19776 if cu % 2 == 0 else 12992)) for cu in range(CU)]
        ck[0] = place((NP0 + 5) * P, R + 25920 - (NP0 + 5) * P)
        ck = [t.rearrange("p (n c) -> p n c", c=P) for t in ck]

        def cmp_arrived(cu):
            return sum(n * PAGES // 2 for c, (_, _, n) in enumerate(cmp_units[:cu + 1]) if c % 2 == cu % 2)

        w2 = place(128, R + 25920).rearrange("p (v e) -> p v e", v=2)
        cbias = sm(2)

        o_acc = place(2048, R).rearrange("p (t c) -> p t c", t=4)
        p_sb = place(1024, R + 2048).rearrange("p (s c) -> p s c", s=2)
        pT = place(1024, R + 3072).rearrange("p (s c) -> p s c", s=2)
        pcT = place(4096, R + 4800).rearrange("p (h q) -> p h q", q=P)
        nmx = place(64, R + 4096)
        rsum = place(64, R + 4160)
        pscale = place(64, R + 4224)
        pc_s = place(256, R + 4288)
        pc_e = place(256, R + 4544)
        kv_pg = place(4 * PAGES * 256, R + 9408).rearrange("p (b n c) -> p b n c", b=4, n=PAGES)
        v_win = place(4 * 512, R).rearrange("p (b n c) -> p b n c", b=4, n=WT)
        pT_win = place(5 * P, R + 2048).rearrange("p (n q) -> p n q", q=P)
        pcT_s = place(P, R + 2688)
        imp = place(32, R + 2816)
        selm = place(32, R + 2848)
        pcs = place(32, R + 2880)
        gs = place(6, R + 2912).rearrange("p (g j) -> p g j", g=2)
        gtmp = place(24, R + 2920)
        sst = place(16, R + 2944)
        selm2 = place(30, R + 2960)
        pT_sel = place(17 * P, R + 3000).rearrange("p (n q) -> p n q", q=P)
        rk = place(900, R + 3000)
        rk2 = place(900, R + 3900)
        so_sb = place(P, R + 9080)
        s_sel = place(PAST + TS, R + 5176)
        s_win = place(WIN + TS, R + 7256)
        kt_sb = place(2 * 512, R + 7800).rearrange("p (s c) -> p s c", s=2)
        qbd = place(256, R + 25920).rearrange("p (b c) -> p b c", b=DB)
        assert R + 9408 + 4 * PAGES * 256 <= R + 25920 and R + 26176 <= ACOLS

        g0 = place(KD * TOK, R).rearrange("p (k t) -> p k t", k=KD)
        g1 = place(KD * TOK, R + 4352).rearrange("p (k t) -> p k t", k=KD)
        mrg = place(KD * TOK, R + 8704).rearrange("p (k t) -> p k t", k=KD)
        x = place(NT * D, R + 21050).rearrange("p (t c) -> p t c", t=NT)
        yT = place(KD * TOK, R + 16650).rearrange("p (k t) -> p k t", k=KD)
        gb = place(D, R + 15600)
        brt = place(2 * TOK, R + 13056).rearrange("p (s t) -> p s t", s=2)
        nrm = place(2 * D, R + 12000).rearrange("p (s c) -> p s c", s=2)
        xj = place(D, R + 14560)
        hid = place(32 * TOK, att0).rearrange("p (k t) -> p k t", k=32)
        assert att0 + 32 * TOK <= R + 13056 and R + 21050 + 5120 <= ACOLS
        memx = place(2 * D, att0).rearrange("p (t c) -> p t c", t=2)
        mnT = place(KD * MEM, att0 + 2048).rearrange("p (k t) -> p k t", k=KD)
        kx = place(2 * 512, att0 + 4096).rearrange("p (t c) -> p t c", t=2)
        vx = place(2 * 512, att0 + 5120).rearrange("p (t c) -> p t c", t=2)
        kxT = place(XH * MEM, att0 + 6144).rearrange("p (h m) -> p h m", h=XH)
        qxT = place(XH * TOK, att0 + 7168).rearrange("p (h t) -> p h t", h=XH)
        oxT = place(XH * TOK, att0 + 9344).rearrange("p (h t) -> p h t", h=XH)
        px = place(2 * 1024, R).rearrange("p (s h m) -> p s h m", s=2, h=XH)
        pxT = place(2 * 1024, R + 2048).rearrange("p (s h m q) -> p s h m q", s=2, h=XH, m=2)
        ox = place(2 * 512, R + 4096).rearrange("p (s c) -> p s c", s=2)
        kxk = place(2 * 2 * 512, R + 5120).rearrange("p (s t c) -> p s t c", s=2, t=2)
        kxv = place(2 * 2 * 512, R + 7168).rearrange("p (s t c) -> p s t c", s=2, t=2)
        kxsT = place(1024, R + 9216).rearrange("p (h m) -> p h m", h=XH)
        qz = place(DB * XH * 32, R + 10240).rearrange("p (b h c) -> p b h c", b=DB, h=XH)
        pxs = place(256, R + 11264)
        pxsT = place(256, R + 11520).rearrange("p (m q) -> p m q", m=2)
        xst = place(64, R + 11800)
        otmp2 = place(1, R + 11864)
        ptmp = place(D, R + 4000)

        def cols(w, c0, n=256):
            return w[:, c0:c0 + n].rearrange("(k p) c -> p k c", p=P)

        w_in = A["w_in"][0]
        o_q, o_kv, o_g, o_m = 512, 1024, 1792, 1816
        chunks = []

        def slot(i, k, n):
            return ring[:, i % RING, 0:k * n].rearrange("p (k c) -> p k c", k=k)

        def add(name, k, n, parts):
            i = len(chunks)
            s = slot(i, k, n)
            chunks.append((name, [(f(s), src) for f, src in parts]))

        whole = lambda s: s
        for c in range(2):
            add(("in", c), KD, 256, [(whole, cols(w_in, c * 256))])
        for c in range(2):
            add(("in", 2 + c), KD, 256,
                [(lambda s, g=g, r=r: s[:, :, r * P + g * HD:r * P + g * HD + HD],
                  cols(w_in, o_q + g * REP * HD + (c * 2 + r) * HD, HD)) for g in range(2) for r in range(2)])
        for c in range(3):
            add(("in", 4 + c), KD, 256, [(whole, cols(w_in, o_kv + c * 256))])
        add(("in", 7), KD, 24, [(whole, cols(w_in, o_g, 24))])
        add(("glu", 0), 4, 512, [(whole, cols(A["w_glu"][0], 0, 512))])
        for c in range(8):
            add(("gate", c), KD, 256, [(whole, cols(w_in, o_m + c * 256))])
        wbn = A["w_br_nsa"][0].rearrange("(g r d) c -> g d r c", g=NKV, r=REP)
        for c in range(2):
            add(("bs", c), 4, 512, [(whole, cols(A["w_br_ssm"][0], c * 512, 512))])
            add(("bn", c), 4, 512,
                [(lambda s, g=g: s[g * HD:(g + 1) * HD], wbn[g, :, :, c * 512:(c + 1) * 512]) for g in range(2)])
        for c in range(4):
            add(("out", c), KD, 256, [(whole, cols(A["w_out"][0], c * 256))])
        for c in range(2):
            add(("xk", c), KD, 256, [(whole, cols(A["w_xk"][0], c * 256))])
        for c in range(2):
            add(("xv", c), KD, 256, [(whole, cols(A["w_xv"][0], c * 256))])
        for c in range(2):
            add(("xq", c), KD, 256, [(whole, cols(A["w_xq"][0], c * 256))])
        for c in range(2):
            add(("xo", c), 4, 512, [(whole, cols(A["w_xo"][0], c * 512, 512))])
        for c in range(16):
            add(("up", c), KD, 256, [(whole, cols(A["w_up"][0], c * 256))])
        for m in range(4):
            for q in range(4):
                add(("down", m * 4 + q), KD, 256,
                    [(whole, cols(A["w_down"][0][q * 1024:(q + 1) * 1024, :], m * 256))])
        index = {name: i for i, (name, _) in enumerate(chunks)}
        arrived, _n = [], [0] * RING
        for i, (_, parts) in enumerate(chunks):
            _n[i % RING] += 16 * len(parts)
            arrived.append(_n[i % RING])
        BC_IN = 38 * 16
        w_sem = [sem(f"weights_{s}") for s in range(RING)]

        units = [("in", m) for m in range(15)] + [("glu", m) for m in range(4)] + [("gate", m) for m in range(16)]
        for m in range(KD):
            units += [("bs", m), ("bn", m)]
        units += [("out", m) for m in range(8)] + [("xq", m) for m in range(4)] + [("xo", m) for m in range(8)]
        units += [("up", m) for m in range(32)]
        unit = {name: i for i, name in enumerate(units)}

        def freed(i):
            kind, c = chunks[i][0]
            if kind in ("xk", "xv"):
                return sem("mem_mm"), 2 * (c + 1) + (4 if kind == "xv" else 0)
            if kind == "down":
                return sem("down_mm"), c + 1
            per = 4 if kind in ("glu", "bs", "bn", "xo") else 2
            return sem("lin_done"), unit[(kind, min(per * c + per - 1, 14) if kind == "in" else per * c + per - 1)] + 1

        outs_done = sem("outputs_stored")
        n_out = [0]

        def store(eng, dst, src):
            eng.dma_start(dst, src).then_inc(outs_done, 16)
            n_out[0] += 16

        CMP1_AT = [7 + 8 * cu for cu in range(CU)]
        CMP2_AT = [at + 3 for at in CMP1_AT]
        assert CMP2_AT[-1] < 64
        S_BANKS = (0, 1, 7)

        once = {
            "tensor":
                "vecs_T lam_T c_T h0_T lags_mm z_mm hfin_T sc_done "
                "kx_T pxs_T",
            "vector":
                "gains_ready half_angles lam_ready lam_out c_out h0_out bp_ready roped "
                "q_roped lags_ready q_read z_out h_ready hfin_ready ssm_states ssm_read "
                "pc_shifted pc_ready prompt_attn_done qbd_ready mem_done x_c_ready qz_ready mxs_done "
                "pxs_ready pxsT_out oxs_out",
            "scalar":
                "dt_ready sines pc_exp pxs_exp",
            "gpsimd":
                "x_zeroed eps_set zrow_set U_zeroed w1_zeroed qbd_zeroed x2_zeroed qz_zeroed",
        }
        step_of = {n: (f"{e}_steps_done", i + 1) for e, names in once.items() for i, n in enumerate(names.split())}
        signalled = {}

        def step(name):
            return sem(step_of[name][0]), step_of[name][1]

        def signal(ins, name, n=1):
            if name in step_of:
                s, at = step_of[name]
                assert signalled.get(s, 0) == at - 1, (name, signalled)
                signalled[s] = at
                ins.then_inc(sem(s), 1)
            else:
                ins.then_inc(sem(name), n)

        class Own:

            def __init__(self, eng, name):
                self.eng, self.sem, self.n = eng, sem(name), 0

            def __call__(self, ins):
                ins.then_inc(self.sem, 1)
                self.n += 1

            def wait(self):
                self.eng.wait_ge(self.sem, self.n)

        def tile_rows(t):
            return P if t < 4 else TS

        def tok0(t):
            return t * P

        def page_numbers(eng, first, n=8):
            return [eng.value_load(page_ids[0:1, bass.ds(first + i, 1)], min_val=0, max_val=NPOOL - 1)
                    for i in range(n)]

        def cmp_pages(eng, cu, half):
            v, s0, n = cmp_units[cu]
            if cu >= 2:
                eng.wait_ge(sem("cmp_done"), cu - 1)
            elif cu == 0:
                eng.wait_ge(sem("y_mm"), 8)
                eng.wait_ge(*step("ssm_states"))
            else:
                eng.wait_ge(sem("yT_T"), 8)
            at = half * n * PAGES // 2
            with eng.Fori(0, n * PAGES // 16) as n8:
                pages = page_numbers(eng, n8 * 8 + (s0 * PAGES + at))
                for i, page in enumerate(pages):
                    eng.dma_start(ck[cu][:, bass.ds(n8 * 8 + (at + i), 1), :],
                                  A["cache_nsa_kv"][0][bass.ds(page, 1), :, v].rearrange("n p g d -> p n (g d)"))\
                        .then_inc(sem(f"cmp_pages_{cu % 2}_{half}"), 16)

        def sel_pages(eng, gg, half):
            if gg == 0:
                eng.wait_ge(sem("cmp_done"), CU)
            for b in range(4):
                if gg:
                    eng.wait_ge(sem("sample_pv"), 4 * (gg - 1) + b + 1)
                pages = page_numbers(eng, (gg * 4 + b) * PAGES + half * 8)
                for i, page in enumerate(pages):
                    eng.dma_start(kv_pg[:, b, half * 8 + i:half * 8 + i + 1, :],
                                  A["cache_nsa_kv"][0][bass.ds(page, 1), :, 2:4].rearrange("n p z g d -> p n (z g d)"))\
                        .then_inc(sem(f"kv_in_{b}_{half}"), 16)

        block = ctx.enter_context(nc.Block())

        @block.sync
        def _(sp):
            nxt = [0]

            def weights(n=1):
                for _ in range(n):
                    i = nxt[0]
                    nxt[0] += 1
                    if i >= RING:
                        sp.wait_ge(*freed(i - RING))
                    for dst, src in chunks[i][1]:
                        sp.dma_start(dst, src).then_inc(w_sem[i % RING], 16)

            sp.dma_start(consts[:, :], A["consts"]).then_inc(sem("consts_in"), 16)
            sp.wait_ge(*step("x_zeroed"))
            for t in range(4):
                sp.dma_start(x_a[:, t, :], A["x_prompt"][0, t * P:(t + 1) * P, :]).then_inc(sem(f"x_in_{t}"), 16)
            sp.dma_start(x_a[0:TS, 4, :], A["x_sample"].rearrange("b q c -> (b q) c")).then_inc(sem("x_in_4"), 16)
            for i, n in enumerate(("g_mix_pre", "g_x_pre", "g_mlp_pre", "g_mem")):
                sp.dma_start(vecs[i * 8:i * 8 + 8, :], A[n][0].rearrange("(k p) -> k p", p=P))\
                    .then_inc(sem("vecs_in"), 16)
            sp.dma_start(vecs[32:36, :], A["b_glu"][0].rearrange("(k p) -> k p", p=P)).then_inc(sem("vecs_in"), 16)
            weights(2)
            for i, n in enumerate(("ssm_lam_re", "ssm_lam_im")):
                sp.dma_start(lamrow[0:GP, i, :], A[n][0].rearrange("(g m) s -> g (m s)", m=2))\
                    .then_inc(sem("lam_in"), 16)
            sp.dma_start(lamrow[0:GP, 2, 0:2], A["ssm_log_dt"][0].rearrange("(g m) -> g m", m=2))\
                .then_inc(sem("lam_in"), 16)
            for z, n in enumerate(("ssm_b_re", "ssm_b_im")):
                v = A[n][0].rearrange("(g m) s c -> m s g c", m=2)
                for m in range(2):
                    sp.dma_start(b_in[m * 64:m * 64 + 64, z], v[m]).then_inc(sem("bc_in"), 16)
            for z, n in enumerate(("ssm_c_re", "ssm_c_im")):
                v = A[n][0].rearrange("(a g m) c s -> a g c m s", a=2, m=2)
                for a in range(2):
                    for g in range(8):
                        sp.dma_start(c_raw[g * 16:g * 16 + 16, z, a, :].rearrange("c (m s) -> c m s", m=2), v[a, g])\
                            .then_inc(sem("bc_in"), 16)
            sp.dma_start(drow[:, :], A["ssm_d"][0].partition_broadcast(P)).then_inc(sem("bc_in"), 16)
            sp.dma_start(h0raw[:, :], A["state_ssm"][0].rearrange("b (g m) s z -> (b g) (m s z)", m=2))\
                .then_inc(sem("bc_in"), 16)
            sp.dma_start(page_ids[:, :], A["page_table"].rearrange("(a b) n -> a (b n)", a=1))\
                .then_inc(sem("pages_in"), 16)
            weights(6)
            weights(1)

            weights(2)

            sp.wait_ge(sem("pages_in"), 16)
            cache = A["cache_nsa_kv"][0]
            for cu in range(CU):
                if cu in (0, 4):
                    v = int(cu > 0)
                    if v:
                        sp.wait_ge(sem("cmp_done"), 3)
                    else:
                        sp.wait_ge(*step("w1_zeroed"))
                    w1 = A[("w_cmpk1", "w_cmpv1")[v]][0].rearrange("(s d) m -> s d m", d=HD)
                    for h in range(2):
                        sp.dma_start(wc[h * 64:h * 64 + 64, :, h * 64:h * 64 + 64], w1).then_inc(sem("w1_in"), 16)
                cmp_pages(sp, cu, 0)
                if cu % 3 == 0:
                    pe = A[("cmp_pe_k", "cmp_pe_v")[cu // 3]][0]
                    for h in range(2):
                        for g in range(2):
                            sp.dma_start(ck[cu][h * 64:h * 64 + 64, NP0 + 4, g * 64:g * 64 + 64], pe)\
                                .then_inc(sem("pe_in"), 16)
                if cu == 0:
                    for v2, name in enumerate(("w_cmpk2", "w_cmpv2")):
                        for h in range(2):
                            sp.dma_start(w2[h * 64:h * 64 + 64, v2, :], A[name][0]).then_inc(sem("w2_in"), 16)

            win = A["cache_win_kv"][0]
            for gg in range(NG2):
                sel_pages(sp, gg, 0)
                if gg == 0:
                    sp.wait_ge(*step("prompt_attn_done"))
                for b in range(4):
                    w = win[gg * 4 + b].rearrange("(n p) z g d -> z p n (g d)", p=P)
                    sp.wait_ge(sem("k_used"), gg * 20 + b + 1)
                    sp.dma_start(kv_pg[:, b, 0:WT, 0:P], w[0]).then_inc(sem(f"k_win_{b}"), 16)
                    sp.dma_start(v_win[:, b], w[1]).then_inc(sem("v_win_in"), 16)

            weights(1)
            sp.wait_ge(sem("sample_pv"), 4 * NG2)
            for t in range(4):
                sp.dma_start(x[:, t, :], A["x_prompt"][0, t * P:(t + 1) * P, :]).then_inc(sem("x2_in"), 16)
            sp.wait_ge(*step("x2_zeroed"))
            sp.dma_start(x[0:TS, 4, :], A["x_sample"].rearrange("b q c -> (b q) c")).then_inc(sem("x2_in"), 16)
            sp.dma_start(gb[:, :], A["g_mix_post"][0].partition_broadcast(P)).then_inc(sem("gb_in"), 16)
            weights(index[("out", 2)] - nxt[0])
            sp.wait_ge(sem("merged"), 8)
            sp.wait_ge(sem("kv_stored"), 64)
            for t in range(2):
                sp.dma_start(memx[:, t, :], A["mem_prompt"][0, t * P:(t + 1) * P, :]).then_inc(sem("mem_in"), 16)
            weights(index[("up", 0)] - nxt[0])
            sp.wait_ge(*step("x_c_ready"))
            for z, (tile, used, arrives) in enumerate(((kxk, "kxs_T", "xs_in"), (kxv, "xs_used", "xs2_in"))):
                for b in range(DB):
                    if b >= 2:
                        sp.wait_ge(sem(used), b - 1)
                    sp.dma_start(tile[:, b % 2], A["cache_mem_kv"][0, b, :, z].rearrange("(t p) h d -> p t (h d)", p=P))\
                        .then_inc(sem(f"{arrives}_{b % 2}"), 16)
            sp.wait_ge(sem("post_norms"), 1)
            sp.dma_start(gb[:, :], A["g_x_post"][0].partition_broadcast(P)).then_inc(sem("gb_in"), 16)
            weights(index[("up", 4)] - nxt[0])
            sp.wait_ge(sem("post_norms"), 2)
            sp.dma_start(gb[:, :], A["g_mlp_post"][0].partition_broadcast(P)).then_inc(sem("gb_in"), 16)
            weights(len(chunks) - nxt[0])
            sp.wait_ge(sem("y_ready"), NT)
            sp.dma_start(y_prompt[0].rearrange("(t p) c -> p t c", p=P), x[:, 0:4, :]).then_inc(sem("y_stored"), 16)
            sp.dma_start(y_sample.rearrange("b q c -> (b q) c"), x[0:TS, 4, :]).then_inc(sem("y_stored"), 16)
            sp.wait_ge(sem("y_stored"), 32)

        @block.gpsimd
        def _(pool):
            signal(pool.memset(x_a[:, 4, :], 0.0), "x_zeroed")
            signal(pool.memset(eps, EPS), "eps_set")
            pool.memset(hz, 0.0)
            signal(pool.memset(zrow[0:112, :], 0.0), "zrow_set")
            for b in range(DB):
                store(pool, win_sample[0, b, 0:WIN - DQ], A["cache_win_kv"][0, b, DQ:WIN])
            pool.wait_ge(*step("zrow_set"))
            pool.dma_start(gk_dram[P:P + 112, :], zrow[0:112, :]).then_inc(sem("gk_out"), 16)
            pool.wait_ge(sem("tok_ready"), 4)
            pool.dma_start(us_dram[0:TP].rearrange("(t p) c -> p t c", p=P), u_tok[:, 0:4, :])\
                .then_inc(sem("us_out"), 16)
            pool.dma_start(us_dram[TP:TOK], u_tok[0:TS, 4, :]).then_inc(sem("us_out"), 16)
            pool.wait_ge(*step("roped"))
            for dst, src in ((kv_prompt[0, 0].rearrange("(t p) z g d -> p t (z g d)", p=P), kvt[:, 0:4, 0:512]),
                             (kv_sample[0].rearrange("b q z g d -> (b q) (z g d)"), kvt[0:TS, 4, 0:512]),
                             (win_prompt[0, 0].rearrange("(t p) z g d -> p t (z g d)", p=P), kvt[:, 0:4, 512:768])):
                pool.dma_start(dst, src).then_inc(sem("kv_stored"), 16)
            for_b = win_sample[0].rearrange("b n z g d -> b n (z g d)")
            pool.dma_start(for_b[:, WIN - DQ:WIN, :], kvt[0:TS, 4, 512:768]).then_inc(sem("kv_stored"), 16)
            pool.wait_ge(*step("q_read"))
            signal(pool.memset(U[64:UROWS], 0.0), "U_zeroed")
            pool.wait_ge(*step("U_zeroed"))
            pool.wait_ge(sem("us_out"), 32)
            us_s = us_dram[TP:TOK].rearrange("(b q) c -> b q c", q=DQ)
            pool.dma_start(U[0:NCH], us_dram[0:TP].rearrange("(n j) c -> n j c", j=L)).then_inc(sem("U_in"), 16)
            pool.dma_start(U[NCH:NCH + DB, 0:DQ], us_s).then_inc(sem("U_in"), 16)
            pool.dma_start(U[NCH + DB:UROWS, DQ:L], us_s).then_inc(sem("U_in"), 16)
            pool.wait_ge(*step("lags_ready"))
            pool.dma_start(gk_dram[0:P, :], G).then_inc(sem("gk_out"), 16)
            pool.wait_ge(sem("gk_out"), 32)
            for i in range(L):
                pool.dma_start(Tz[:, i, :], gk_dram[i * C_SSM:i * C_SSM + P, :]).then_inc(sem("T_in"), 16)
            pool.wait_ge(*step("ssm_states"))
            store(pool, ssm_prompt[0, 0].rearrange("(g m) s z -> g (m s z)", m=2), hout[0:GP, 0:256])
            store(pool, ssm_sample[0].rearrange("b (g m) s z -> (b g) (m s z)", m=2), hout[:, 256:512])
            pool.wait_ge(outs_done, n_out[0])
            pool.wait_ge(sem("y_mm"), 8)
            pool.memset(wc[0:64, :, 64:P], 0.0)
            signal(pool.memset(wc[64:P, :, 0:64], 0.0), "w1_zeroed")
            pool.wait_ge(sem("pages_in"), 16)
            for cu in range(CU):
                cmp_pages(pool, cu, 1)
            pool.wait_ge(sem("cmp2_mm"), CU)
            signal(pool.memset(qbd, 0.0), "qbd_zeroed")
            for gg in range(NG2):
                sel_pages(pool, gg, 1)
            pool.wait_ge(sem("sample_pv"), 4 * NG2)
            signal(pool.memset(x[:, 4, :], 0.0), "x2_zeroed")
            pool.wait_ge(*step("x_c_ready"))
            signal(pool.memset(qz, 0.0), "qz_zeroed")
            pool.wait_ge(*step("mem_done"))
            mkv = mem_kv_prompt[0, 0].rearrange("(t p) z h d -> z p t (h d)", p=P)
            for z, tile in enumerate((kx, vx)):
                pool.dma_start(mkv[z], tile).then_inc(sem("mem_stored"), 16)
            pool.wait_ge(sem("mem_stored"), 32)
            pool.wait_ge(sem("kv_stored"), 64)
            pool.wait_ge(outs_done, n_out[0])

        @block.tensor
        def _(pe):
            own = Own(pe, "pe_steps")
            mm = pe.matmul

            def done_unit(name):
                return 2 * (unit[name] + 1)

            def linear(name, lhsT, rhs, K, M=P, last_of=None):
                u = unit[name]
                if u >= 2:
                    pe.wait_ge(sem("lin_out"), 2 * (u - 1))
                b = 2 * (u % 2)
                for k in range(K):
                    for h in range(2):
                        ins = mm(bank(b + h, HALF, rows=M), lhsT(k), rhs[:, k, h * HALF:(h + 1) * HALF],
                                 start=(k == 0), stop=(k == K - 1))
                signal(ins, "lin_done")

            def chunk(name, k, n):
                i = index[name]
                pe.wait_ge(w_sem[i % RING], arrived[i])
                return slot(i, k, n)

            def prenorm_T(tag, ntiles):
                for t in range(ntiles):
                    pe.wait_ge(sem(f"xn_{tag}"), t + 1)
                    if t >= 2:
                        pe.wait_ge(sem(f"xT_{tag}"), t - 1)
                    n = tile_rows(t) if tag != "mem" else P
                    src = nrm if tag != "mix" else xn
                    for k in range(KD):
                        ins = pe.transpose(bank(4 + 2 * (t % 2) + k // 4, n, (k % 4) * P), src[0:n, t % 2, k * P:(k + 1) * P],
                                           ident[0:n, 0:n])
                    signal(ins, f"xt_{tag}")

            pe.wait_ge(sem("consts_in"), 16)
            pe.wait_ge(sem("vecs_in"), 80)
            signal(pe.transpose(bank(0, 36), vecs[0:36, :], ident[0:36, 0:36]), "vecs_T")
            prenorm_T("mix", NT)
            pe.wait_ge(*step("gains_ready"))
            pe.wait_ge(sem("xT_mix"), NT)

            def back(m):
                M = 24 if m == 14 else P
                pe.wait_ge(sem("lin_out"), done_unit(("in", m)))
                if m >= 2:
                    pe.wait_ge(sem("tok_ready"), m - 1)
                f = fT[:, m % 2]
                for t in range(NT):
                    n = tile_rows(t)
                    ins = pe.transpose(bank(4 + 2 * (m % 2) + t // 4, M, (t % 4) * P, rows=n),
                                       f[0:M, tok0(t):tok0(t) + n], ident[0:M, 0:M])
                signal(ins, "back_T")

            for m in range(15):
                c = chunk(("in", m // 2), KD, 256 if m < 14 else 24)
                if m == 14:
                    linear(("in", m), lambda k: c[:, k, 0:24], actT, KD, 24)
                else:
                    linear(("in", m), lambda k: c[:, k, (m % 2) * P:(m % 2) * P + P], actT, KD)
                if m >= 1:
                    back(m - 1)
                if m == 2:
                    pe.wait_ge(*step("lam_ready"))
                    pe.wait_ge(sem("tok_ready"), 2)
                    for v in range(7):
                        ins = pe.transpose(bank(7, GP, 256 + v * GP), lamrow[0:GP, v, :], ident[0:GP, 0:GP])
                    signal(ins, "lam_T")
                    pe.wait_ge(*step("lam_out"))
                    pe.wait_ge(sem("bc_in"), BC_IN)
                    for z in range(2):
                        for a in range(2):
                            ins = pe.transpose(bank(7, P, (z * 2 + a) * P), c_raw[:, z, a, :], ident)
                    signal(ins, "c_T")
                    pe.wait_ge(*step("c_out"))
                    for z in range(2):
                        ins = pe.transpose(bank(7, P, z * P), h0raw.rearrange("p (s z) -> p z s", z=2)[:, z], ident)
                    signal(ins, "h0_T")
                    pe.wait_ge(*step("h0_out"))
            back(14)

            pe.wait_ge(sem("tok_ready"), 15)
            for n in range(8):
                if n == 0:
                    pe.wait_ge(*step("bp_ready"))
                if n >= 2:
                    pe.wait_ge(sem("m1_out"), n - 1)
                for i in range(4):
                    q = n * 4 + i
                    ins = pe.transpose(bank(4 + n % 2, P, i * P), BP[:, q // GP, q % GP], ident)
                signal(ins, "m1_T")
            for g in range(GP):
                for z in range(2):
                    ins = mm(bank(6, 32, g * 32), BP[:, z, g], cblk[:, z, g], start=(z == 0), stop=(z == 1))
            signal(ins, "lags_mm")

            pe.wait_ge(*step("roped"))
            pe.wait_ge(*step("q_roped"))
            pe.wait_ge(sem("m1_out"), 8)
            srcs = [q_tok[:, :, r * P:(r + 1) * P] for r in range(REP)] + [kvt[:, :, 256:384], kvt[:, :, 512:640]]
            for i, s in enumerate(srcs):
                if i >= 2:
                    pe.wait_ge(sem("qk_out"), i - 1)
                for t in range(4):
                    pe.transpose(bank(4 + i % 2, P, t * P), s[:, t, :], ident)
                ins = pe.transpose(bank(7, TS, i * TS), s[0:TS, 4, :], ident[0:TS, 0:TS])
                signal(ins, "qk_T")

            pe.wait_ge(sem("U2_ready"), 2)
            pe.wait_ge(*step("lags_ready"))
            pe.wait_ge(sem("qk_out"), 7)
            for n in range(6):
                if n >= 2:
                    pe.wait_ge(sem("ut_out"), n - 1)
                for g in range(n * 6, min(n * 6 + 6, G_SSM)):
                    ins = pe.transpose(bank(6 + n % 2, UROWS, (g - n * 6) * UROWS),
                                       U2[g // 16][0:UROWS, g % 16, :], ident[0:UROWS, 0:UROWS])
                signal(ins, "ut_T")
            pe.wait_ge(sem("ut_out"), 6)
            pe.wait_ge(sem("lin_out"), done_unit(("in", 14)))
            for z in range(2):
                for g in range(G_SSM):
                    gp, m = g // 2, g % 2
                    out = psum[m * 64:m * 64 + 64, z * 3 + gp // 6, (gp % 6) * UROWS:(gp % 6 + 1) * UROWS]
                    ins = mm(out, M1[:, z, gp, m * 64:m * 64 + 64], UT[:, g, :], start=True, stop=True)
            signal(ins, "z_mm")
            pe.wait_ge(sem("T_in"), 128)
            pe.wait_ge(*step("h_ready"))
            for n in range(8):
                if n == 0:
                    pe.wait_ge(*step("z_out"))
                if n >= 2:
                    pe.wait_ge(sem("y_out"), n - 1)
                for i in range(4):
                    gp, m = n // 2 * 4 + i, n % 2
                    g = 2 * gp + m
                    out = bank(6 + n % 2, P, i * P, rows=YROWS)
                    mm(out, UT[:, g, 0:YROWS], Tz[:, :, g * C_SSM:(g + 1) * C_SSM], start=True, stop=False)
                    for z in range(2):
                        ins = mm(out, Z[m * 64:m * 64 + 64, z, gp, 0:YROWS], M2[m * 64:m * 64 + 64, z, gp],
                                 start=False, stop=(z == 1))
                signal(ins, "y_mm")
            pe.wait_ge(*step("hfin_ready"))
            for z in range(2):
                pe.transpose(bank(4, P, z * P, rows=GP), hfp[:, z], ident)
                ins = pe.transpose(bank(4, P, 256 + z * P), hfs[:, z], ident)
            signal(ins, "hfin_T")
            pe.wait_ge(sem("y_out"), 8)
            pe.wait_ge(*step("ssm_states"))
            for n in range(8):
                if n >= 2:
                    pe.wait_ge(sem("yT_out"), n - 1)
                ct, half = n // 2, n % 2
                for j in range(4):
                    i = half * 4 + j
                    ins = pe.transpose(bank(4 + n % 2, YROWS, j * YROWS), y_sb[0:YROWS, L - 1 - i, ct * P:(ct + 1) * P],
                                       ident[0:YROWS, 0:YROWS])
                signal(ins, "yT_T")
            pe.wait_ge(sem("yT_out"), 8)
            c = chunk(("glu", 0), 4, 512)
            for m in range(4):
                linear(("glu", m), lambda k: c[:, k, m * P:(m + 1) * P], yg, 4)

            def cmp1(cu):
                (v, s0, ns), first = cmp_units[cu], cu % 3 == 0
                pe.wait_ge(sem("w1_in"), 32 * (v + 1))
                for half in range(2):
                    pe.wait_ge(sem(f"cmp_pages_{cu % 2}_{half}"), 16 * cmp_arrived(cu))
                n = NP0 + 5 if first else ns * PAGES
                if first:
                    pe.wait_ge(sem("prompt_rows"), v + 1)
                    pe.wait_ge(sem("pe_in"), 64 * (v + 1))
                if cu >= 1:
                    pe.wait_ge(sem("hz_ready"), cu)
                rows = ck[cu].rearrange("p n (g d) -> p n g d", g=2)
                for d in range(HD):
                    ins = mm(bank(6, 2 * n), wc[:, d, :], rows[:, 0:n, :, d], start=(d == 0), stop=(d == HD - 1))
                signal(ins, "cmp_done")

            def cmp2(cu):
                (v, s0, ns), first = cmp_units[cu], cu % 3 == 0
                pe.wait_ge(sem("hz_ready"), cu + 1)
                pe.wait_ge(sem("w2_in"), 64)
                w2v = w2[:, v, :]
                h = hz[:, cu % 2]
                if cu >= 1:
                    pe.wait_ge(sem("cmp_out"), cu)
                if v == 0:
                    n = NP0 + 4 if first else ns * PAGES
                    for g in range(2):
                        ins = mm(psum[g * 64:g * 64 + 64, 6, P:P + 2 * n], w2v, h[:, g, 0:n, :], start=True, stop=True)
                else:
                    for b in range(ns):
                        for g in range(2):
                            ins = mm(bank(6, 64, P + (b * 2 + g) * 64, rows=32), h[:, g, b * PAGES:(b + 1) * PAGES, :], w2v,
                                     start=True, stop=True)
                    if first:
                        for g in range(2):
                            ins = mm(bank(6, 64, P + 256 + g * 64, rows=8), h[:, g, NP0:NP0 + 4, :], w2v, start=True, stop=True)
                signal(ins, "cmp2_mm")

            pe.wait_ge(*step("ssm_read"))
            N = 64
            for i in range(N + 3):
                if i < N:
                    br, qt, r, g = i // 32, i // 8 % 4, i // 2 % 4, i % 2
                    if i >= 3:
                        pe.wait_ge(sem("p_ready"), i - 2)
                    s = slice(g * 64, g * 64 + 64)
                    signal(mm(bank(S_BANKS[i % 3], (qt + 1) * P), qT[s, r, qt * P:(qt + 1) * P], kT[s, br, 0:(qt + 1) * P],
                              start=True, stop=True), "s_done")
                if 2 <= i < N + 2:
                    j = i - 2
                    qt = j // 8 % 4
                    pe.wait_ge(sem("p_ready"), j + 1)
                    if j >= 2:
                        pe.wait_ge(sem("pT_ready"), j - 1)
                    for kt in range(qt + 1):
                        ins = pe.transpose(bank(2 + j % 2, P, kt * P), p_sb[:, j % 2, kt * P:(kt + 1) * P], ident)
                    signal(ins, "p_T")
                if i >= 3:
                    j = i - 3
                    br, qt, r, g = j // 32, j // 8 % 4, j // 2 % 4, j % 2
                    pe.wait_ge(sem("pT_ready"), j + 1)
                    if j % 8 == 0 and j >= 16:
                        pe.wait_ge(sem("o_taken"), j // 8 - 1)
                    vcol = (384, 640)[br] + g * 64
                    for kt in range(qt + 1):
                        ins = mm(bank(4 + j // 8 % 2, 64, (j % 8) * 64), pT[:, j % 2, kt * P:(kt + 1) * P],
                                 kvt[:, kt, vcol:vcol + 64], start=(kt == 0), stop=(kt == qt))
                    signal(ins, "pv_done")
                if i in CMP1_AT:
                    cmp1(CMP1_AT.index(i))
                if i in CMP2_AT:
                    cmp2(CMP2_AT.index(i))
            pe.wait_ge(sem("cmp_out"), CU)
            for qt in range(4):
                for r in range(REP):
                    for g in range(2):
                        s = slice(g * 64, g * 64 + 64)
                        ins = mm(bank(g, 8, qt * 32 + r * 8), qT[s, r, qt * P:(qt + 1) * P], kcT[s, 256:264],
                                 start=True, stop=True)
            signal(ins, "sc_done")
            pe.wait_ge(*step("pc_ready"))
            for n in range(8):
                if n >= 2:
                    pe.wait_ge(sem("pcT_out"), n - 1)
                for i in range(4):
                    h = n * 4 + i
                    ins = pe.transpose(bank(2 + n % 2, P, i * P, rows=8), pc_s[:, h * 8:h * 8 + 8], ident)
                signal(ins, "pc_T")
            for qt in range(4):
                pe.wait_ge(sem("pcT_out"), 2 * qt + 2)
                pe.wait_ge(sem("o_taken"), 7 + qt)
                for h in range(8):
                    ins = mm(bank(4 + qt % 2, 64, h * 64), pcT[0:8, qt * 8 + h, :], vcp[0:8, (h % 2) * 64:(h % 2) * 64 + 64],
                             start=True, stop=True)
                signal(ins, "pv_done")
            for qt in range(4):
                pe.wait_ge(sem("o_taken"), 9 + qt)
                if qt >= 2:
                    pe.wait_ge(sem("nsa_out"), qt - 1)
                for r in range(REP):
                    ins = pe.transpose(bank(6 + qt % 2, P, r * P), o_acc[:, qt, r * P:(r + 1) * P], ident)
                signal(ins, "o_T")
            pe.wait_ge(sem("nsa_out"), 4)

            for gg in range(NG2):
                if gg:
                    pe.wait_ge(sem("nsa_s_out"), gg)
                signal(mm(bank(6, 24), C("spread")[0:TS, gg * P:(gg + 1) * P], gtk[0:TS, 4, :], start=True, stop=True),
                       "gs_mm")
                pe.wait_ge(*step("qbd_ready"))
                for b in range(4):
                    ins = mm(psum[b * 32:b * 32 + 32, 7, 0:32], qbd[:, gg * 4 + b, :],
                             kcT[:, (gg * 4 + b) * 32:(gg * 4 + b) * 32 + 32], start=True, stop=True)
                signal(ins, "sc_s_mm")
                pe.wait_ge(sem("pc_s_ready"), gg + 1)
                signal(mm(bank(6, 32, 64), C("rows4"), pcs, start=True, stop=True), "imp_mm")
                for u in range(20 + 1):
                    if u < 20:
                        kc, b, U_ = u // 4, u % 4, gg * 20 + u
                        if kc == 4:
                            pe.wait_ge(sem(f"k_win_{b}"), 16 * (gg + 1))
                        else:
                            pe.wait_ge(sem(f"kv_in_{b}_{kc // 2}"), 16 * 8 * (gg + 1))
                        n0 = kc % 4 * 4
                        if U_ >= 2:
                            pe.wait_ge(sem("kt_out"), U_ - 1)
                        for i in range(4):
                            ins = pe.transpose(bank(U_ % 2, P, i * P), kv_pg[:, b, n0 + i, 0:P], ident)
                        signal(ins, "k_used")
                    if u >= 1:
                        kc, b, U_ = (u - 1) // 4, (u - 1) % 4, gg * 20 + u - 1
                        pe.wait_ge(sem("kt_out"), U_ + 1)
                        n4 = gg * 5 + kc
                        if b == 0 and n4 >= 2:
                            pe.wait_ge(sem("s_out"), n4 - 1)
                        signal(mm(psum[b * 32:b * 32 + 32, 2 + n4 % 2, :], qbd[:, gg * 4 + b, :], kt_sb[:, U_ % 2, :],
                                  start=True, stop=True), "s_mm")
                for br in range(2):
                    for b in range(4):
                        ins = mm(psum[b * 32:b * 32 + 32, 6, 128 + br * 32:160 + br * 32], qbd[:, gg * 4 + b, :],
                                 kT[:, br, TP:TOK], start=True, stop=True)
                signal(ins, "snew_mm")
                pe.wait_ge(sem("pcg_ready"), gg + 1)
                signal(pe.transpose(bank(7, P, 64, rows=32), pcs, ident), "pcs_T")
                for n in range(6):
                    if n == 0:
                        pe.wait_ge(sem("p_sel"), gg + 1)
                    if n == 4:
                        pe.wait_ge(sem("p_win"), gg + 1)
                    q = gg * 6 + n
                    if q >= 2:
                        pe.wait_ge(sem("ps_out"), q - 1)
                    b_ = 4 + q % 2
                    if n < 4:
                        for i in range(4):
                            ins = pe.transpose(bank(b_, P, i * P), s_sel[:, (n * 4 + i) * P:(n * 4 + i + 1) * P], ident)
                    elif n == 4:
                        pe.transpose(bank(b_, P, 0, rows=TS), s_sel[:, PAST:PAST + TS], ident)
                        ins = pe.transpose(bank(b_, P, P, rows=TS), s_win[:, WIN:WIN + TS], ident)
                    else:
                        for i in range(4):
                            ins = pe.transpose(bank(b_, P, i * P), s_win[:, i * P:(i + 1) * P], ident)
                    signal(ins, "ps_T")
                pe.wait_ge(sem("ps_out"), gg * 6 + 6)
                pe.wait_ge(sem("v_win_in"), 64 * (gg + 1))
                pe.wait_ge(sem("pcs_out"), gg + 1)
                for b in range(4):
                    out = psum[b * 32:b * 32 + 32, 7, 256:384]
                    c32 = slice(b * 32, b * 32 + 32)
                    mm(out, pcT_s[0:32, c32], vc[0:32, gg * 4 + b, :], start=True, stop=False)
                    mm(out, pT_sel[0:TS, 16, c32], kvt[0:TS, 4, 384:512], start=False, stop=False)
                    mm(out, pT_win[0:TS, 4, c32], kvt[0:TS, 4, 640:768], start=False, stop=False)
                    for i in range(PAGES):
                        mm(out, pT_sel[:, i, c32], kv_pg[:, b, i, P:256], start=False, stop=False)
                    for i in range(WT):
                        ins = mm(out, pT_win[:, i, c32], v_win[:, b, i, :], start=False, stop=(i == WT - 1))
                    signal(ins, "sample_pv")
                pe.wait_ge(sem("so_out"), gg + 1)
                signal(pe.transpose(bank(7, P, 384), so_sb, ident), "so_T")
            pe.wait_ge(sem("nsa_s_out"), 2)

            for m in range(16):
                c = chunk(("gate", m // 2), KD, 256)
                linear(("gate", m), lambda k: c[:, k, (m % 2) * P:(m % 2) * P + P], actT, KD)
            for m in range(KD):
                for kind, act in (("bs", ssmT), ("bn", nsaT)):
                    c = chunk((kind, m // 4), 4, 512)
                    linear((kind, m), lambda k: c[:, k, (m % 4) * P:(m % 4) * P + P], act, 4)
            pe.wait_ge(sem("merged"), 8)
            for m in range(8):
                c = chunk(("out", m // 2), KD, 256)
                linear(("out", m), lambda k: c[:, k, (m % 2) * P:(m % 2) * P + P], mrg, KD)

            def postnorm_T(i, ready):
                for t in range(NT):
                    if t == 0:
                        pe.wait_ge(*ready)
                    if t >= 2:
                        pe.wait_ge(sem("post_added"), i * NT + t - 1)
                    n = tile_rows(t)
                    for k in range(KD):
                        ins = pe.transpose(bank(4 + 2 * (t % 2) + k // 4, P, (k % 4) * P, rows=n),
                                           yT[:, k, tok0(t):tok0(t) + n], ident)
                    signal(ins, "post_T")

            prenorm_T("mem", 2)
            pe.wait_ge(sem("xT_mem"), 2)
            for i in range(8):
                kind, c, t = ("xk", "xv")[i // 4], i // 2 % 2, i % 2
                w = chunk((kind, c), KD, 256)
                if i >= 2:
                    pe.wait_ge(sem("mem_out"), i - 1)
                for k in range(KD):
                    ins = mm(bank(4 + i % 2, 256), mnT[:, k, t * P:(t + 1) * P], w[:, k, :], start=(k == 0), stop=(k == KD - 1))
                signal(ins, "mem_mm")
            pe.wait_ge(sem("mem_out"), 8)
            for h in range(XH):
                for t in range(2):
                    ins = pe.transpose(bank(6 + h // 2, P, (h % 2) * 256 + t * P), kx[:, t, h * P:(h + 1) * P], ident)
            signal(ins, "kx_T")

            pe.wait_ge(sem("kxT_out"), 2)
            postnorm_T(0, (sem("lin_out"), done_unit(("out", 7))))
            pe.wait_ge(sem("post_added"), NT)
            prenorm_T("x", NT)
            pe.wait_ge(sem("xT_x"), NT)
            for m in range(4):
                c = chunk(("xq", m // 2), KD, 256)
                linear(("xq", m), lambda k: c[:, k, (m % 2) * P:(m % 2) * P + P], actT, KD)
            pe.wait_ge(sem("lin_out"), done_unit(("xq", 3)))
            for i in range(6):
                if i < 4:
                    if i >= 1:
                        pe.wait_ge(sem("px_exp"), 4 * i)
                    for h in range(XH):
                        ins = mm(bank(h // 2, 256, (h % 2) * 256), qxT[:, h, i * P:(i + 1) * P], kxT[:, h, :],
                                 start=True, stop=True)
                    signal(ins, "sx_done")
                if 1 <= i <= 4:
                    j = i - 1
                    pe.wait_ge(sem("px_exp"), 4 * i)
                    if j >= 1:
                        pe.wait_ge(sem("pxT_out"), 2 * j)
                    for h in range(XH):
                        for m in range(2):
                            ins = pe.transpose(bank(2 + h // 2, P, (h % 2) * 256 + m * P), px[:, j % 2, h, m * P:(m + 1) * P], ident)
                    signal(ins, "px_T")
                    pe.wait_ge(sem("pxT_out"), 2 * i)
                    if j >= 2:
                        pe.wait_ge(sem("ox_norm"), j - 1)
                    for h in range(XH):
                        for m in range(2):
                            ins = mm(bank(4 + j % 2, P, h * P), pxT[:, j % 2, h, m, :], vx[:, m, h * P:(h + 1) * P],
                                     start=(m == 0), stop=(m == 1))
                    signal(ins, "ox_mm")
                if i >= 2:
                    j = i - 2
                    pe.wait_ge(sem("ox_norm"), j + 1)
                    if j >= 1:
                        pe.wait_ge(sem("oxT_out"), j)
                    for h in range(XH):
                        ins = pe.transpose(bank(6, P, h * P), ox[:, j % 2, h * P:(h + 1) * P], ident)
                    signal(ins, "ox_T")
            pe.wait_ge(*step("qz_ready"))
            for b in range(DB):
                pe.wait_ge(sem(f"xs_in_{b % 2}"), 16 * (b // 2 + 1))
                if b >= 1:
                    pe.wait_ge(sem("kxsT_out"), 2 * b)
                for h in range(XH):
                    for m in range(2):
                        ins = pe.transpose(bank(h // 2, P, (h % 2) * 256 + m * P), kxk[:, b % 2, m, h * P:(h + 1) * P], ident)
                signal(ins, "kxs_T")
                pe.wait_ge(sem("kxsT_out"), 2 * b + 2)
                for h in range(XH):
                    q = b // 2 * 32
                    ins = mm(psum[q:q + 32, 7, 0:256], qz[:, b, h, :], kxsT[:, h, :],
                             start=(b % 2 == 0 and h == 0), stop=(b % 2 == 1 and h == XH - 1))
                signal(ins, "kxs_mm")
            pe.wait_ge(*step("pxs_ready"))
            for m in range(2):
                ins = pe.transpose(bank(7, P, 256 + m * P), pxs[:, m * P:(m + 1) * P], ident)
            signal(ins, "pxs_T")
            pe.wait_ge(*step("pxsT_out"))
            pe.wait_ge(sem("oxT_out"), 4)
            for b in range(DB):
                pe.wait_ge(sem(f"xs2_in_{b % 2}"), 16 * (b // 2 + 1))
                for h in range(XH):
                    for m in range(2):
                        ins = mm(bank(6, DQ, h * TS + b * DQ), kxv[:, b % 2, m, h * P:(h + 1) * P],
                                 pxsT[:, m, (b * XH + h) * DQ:(b * XH + h + 1) * DQ], start=(m == 0), stop=(m == 1))
                signal(ins, "xs_used")
            pe.wait_ge(*step("oxs_out"))
            for m in range(8):
                c = chunk(("xo", m // 4), 4, 512)
                linear(("xo", m), lambda k: c[:, k, (m % 4) * P:(m % 4) * P + P], oxT, 4)
            postnorm_T(1, (sem("lin_out"), done_unit(("xo", 7))))
            pe.wait_ge(sem("post_added"), 2 * NT)
            prenorm_T("mlp", NT)
            pe.wait_ge(sem("xT_mlp"), NT)
            for m in range(32):
                c = chunk(("up", m // 2), KD, 256)
                linear(("up", m), lambda k: c[:, k, (m % 2) * P:(m % 2) * P + P], actT, KD)
            pe.wait_ge(sem("hid_ready"), 64)
            for m in range(4):
                if m >= 2:
                    pe.wait_ge(sem("down_out"), 4 * (m - 1))
                for q in range(4):
                    c = chunk(("down", m * 4 + q), KD, 256)
                    for k in range(KD):
                        for j in range(2):
                            for h in range(2):
                                ins = mm(bank(4 * (m % 2) + 2 * j + h, HALF), c[:, k, j * P:(j + 1) * P],
                                         hid[:, q * KD + k, h * HALF:(h + 1) * HALF],
                                         start=(q == 0 and k == 0), stop=(q == 3 and k == KD - 1))
                    signal(ins, "down_mm")
            postnorm_T(2, (sem("down_out"), 16))

        @block.scalar
        def _(act):
            own = Own(act, "act_steps")
            fn = act.activation

            act.wait_ge(*step("eps_set"))
            for t in range(NT):
                act.wait_ge(sem(f"x_in_{t}"), 16)
                own(fn(junk, x_a[:, t, :], ACT.Square, accum_out=ssq[:, t:t + 1]))
                own.wait()
                signal(fn(rms[:, t:t + 1], ssq[:, t:t + 1], ACT.Sqrt, bias=eps, scale=1.0 / D), "rms_mix")

            lr = lamrow
            act.wait_ge(sem("lam_in"), 48)
            signal(fn(lr[0:GP, 2, 0:2], lr[0:GP, 2, 0:2], ACT.Exp), "dt_ready")

            def take(name, f, M=P):
                u = unit[name]
                act.wait_ge(sem("lin_done"), u + 1)
                for h in range(2):
                    signal(f(h, bank(2 * (u % 2) + h, HALF, rows=M), slice(h * HALF, (h + 1) * HALF)), "lin_out")

            for m in range(15):
                if m == 1:
                    act.wait_ge(*step("half_angles"))
                    own(fn(lr[0:GP, 10, :], lr[0:GP, 8, :], ACT.Sin))
                    signal(fn(lr[0:GP, 11, :], lr[0:GP, 9, :], ACT.Sin), "sines")
                if m >= 2:
                    act.wait_ge(sem("back_T"), m - 1)
                if m < 14:
                    take(("in", m), lambda h, ps, s: fn(fT[:, m % 2, s], ps, ACT.Copy))
                else:
                    take(("in", m), lambda h, ps, s: fn(fT[0:24, m % 2, s], ps, ACT.Sigmoid), 24)
            act.wait_ge(sem("U_in"), 48)
            act.wait_ge(sem("back_T"), 15)
            for a in range(2):
                signal(fn(U2[a][0:UROWS].rearrange("p g (j c) -> p g j c", c=C_SSM),
                          U[0:UROWS, :, a * 256:(a + 1) * 256].rearrange("p j (g c) -> p g j c", c=C_SSM), ACT.Copy), "U2_ready")
            for n in range(8):
                ct, half = n // 2, n % 2
                act.wait_ge(sem("yT_T"), n + 1)
                if n == 0:
                    act.wait_ge(*step("ssm_states"))
                ps = bank(4 + n % 2, 4 * YROWS).rearrange("p (i n) -> p i n", i=4)
                if half == 0:
                    own(fn(yg[:, ct, TP:TOK].rearrange("p (b i) -> p i b", i=DQ), ps[:, :, NCH:YROWS], ACT.Gelu_apprx_tanh))
                signal(fn(yg[:, ct, 0:TP].rearrange("p (n i) -> p i n", i=L)[:, half * 4:half * 4 + 4, :],
                          ps[:, :, 0:NCH], ACT.Gelu_apprx_tanh), "yT_out")
            for m in range(4):
                take(("glu", m), lambda h, ps, s: fn(sg[:, m, s], ps, ACT.Sigmoid, bias=bglu[:, m:m + 1]))

            def cmp_gelu(cu):
                (v, s0, ns), first = cmp_units[cu], cu % 3 == 0
                act.wait_ge(sem("cmp_done"), cu + 1)
                if first:
                    own(fn(cbias[:, v:v + 1], bank(6, 1, 2 * (NP0 + 4)), ACT.Copy))
                    own.wait()
                if cu >= 2:
                    act.wait_ge(sem("cmp2_mm"), cu - 1)
                n = NP0 + 4 if first else ns * PAGES
                for h in range(2):
                    rows = slice(h * 64, h * 64 + 64)
                    ins = fn(hz[rows, cu % 2, :, 0:n, h].rearrange("p g n -> p n g"),
                             psum[rows, 6, 0:2 * n].rearrange("p (n g) -> p n g", g=2),
                             ACT.Gelu_apprx_tanh, bias=cbias[rows, v:v + 1])
                    if h == 0:
                        own(ins)
                    else:
                        signal(ins, "hz_ready")

            for i in range(64):
                qt = i // 8 % 4
                act.wait_ge(sem("mx_done"), i + 1)
                if i >= 2:
                    act.wait_ge(sem("p_T"), i - 1)
                n = (qt + 1) * P
                signal(fn(p_sb[:, i % 2, 0:n], bank(S_BANKS[i % 3], n), ACT.Exp, bias=nmx[:, i:i + 1],
                          accum_out=rsum[:, i:i + 1]), "p_ready")
                if i - 1 in CMP1_AT:
                    cmp_gelu(CMP1_AT.index(i - 1))
            act.wait_ge(*step("pc_shifted"))
            signal(fn(pc_e, pc_s, ACT.Exp), "pc_exp")
            for gg in range(NG2):
                act.wait_ge(sem("pcs_max"), gg + 1)
                signal(fn(pcs, bank(7, 32), ACT.Exp, bias=sst[:, 0:1], accum_out=sst[:, 1:2]), "pcs_exp")
                for u in range(20):
                    U_ = gg * 20 + u
                    act.wait_ge(sem("k_used"), U_ + 1)
                    if U_ >= 2:
                        act.wait_ge(sem("s_mm"), U_ - 1)
                    signal(fn(kt_sb[:, U_ % 2, :], bank(U_ % 2), ACT.Copy), "kt_out")
                act.wait_ge(sem("sel_max"), gg + 1)
                signal(fn(s_sel, s_sel, ACT.Exp, bias=sst[:, 2:3], accum_out=sst[:, 3:4]), "sel_exp")
                signal(fn(s_win, s_win, ACT.Exp, bias=sst[:, 4:5], accum_out=sst[:, 5:6]), "sel_exp")

            for m in range(16):
                dst = g0 if m < 8 else g1
                if m == 0:
                    act.wait_ge(sem("nsa_s_out"), 2)
                take(("gate", m), lambda h, ps, s: fn(dst[:, m % 8, s], ps, ACT.Sigmoid))
            for m in range(KD):
                for j, kind in enumerate(("bs", "bn")):
                    if m >= 1:
                        act.wait_ge(sem("merged"), m)
                    take((kind, m), lambda h, ps, s: fn(brt[:, j, s], ps, ACT.Copy))

            def rms_of(tag, src, t, j, wait):
                act.wait_ge(*wait)
                n = P if tag == "mem" else tile_rows(t)
                own(fn(xj[0:n, :], src, ACT.Square, accum_out=ssq[0:n, j:j + 1]))
                own.wait()
                signal(fn(rms[0:n, j:j + 1], ssq[0:n, j:j + 1], ACT.Sqrt, bias=eps[0:n], scale=1.0 / D), f"rms_{tag}")

            def post(i):
                for t in range(NT):
                    n = tile_rows(t)
                    rms_of("post", psum[0:n, 4 + 2 * (t % 2):6 + 2 * (t % 2), :].rearrange("p b c -> p (b c)"), t, t,
                           (sem("post_T"), i * NT + t + 1))
                    if i < 2:
                        rms_of(("x", "mlp")[i], x[0:n, t, :], t, 8 + t, (sem("post_added"), i * NT + t + 1))

            for m in range(8):
                take(("out", m), lambda h, ps, s: fn(yT[:, m, s], ps, ACT.Copy))
            for t in range(2):
                rms_of("mem", memx[:, t, :], t, 5 + t, (sem("mem_in"), 32))
            post(0)
            for m in range(4):
                take(("xq", m), lambda h, ps, s: fn(qxT[:, m, s], ps, ACT.Copy, scale=XD ** -0.5))
            for i in range(4):
                act.wait_ge(sem("mxx_done"), i + 1)
                if i >= 2:
                    act.wait_ge(sem("px_T"), i - 1)
                for h in range(XH):
                    signal(fn(px[:, i % 2, h, :], bank(h // 2, 256, (h % 2) * 256), ACT.Exp,
                              bias=xst[:, i * 8 + h:i * 8 + h + 1], accum_out=xst[:, i * 8 + 4 + h:i * 8 + 5 + h]), "px_exp")
            act.wait_ge(*step("mxs_done"))
            signal(fn(pxs, bank(7, 256), ACT.Exp, bias=xst[:, 32:33], accum_out=xst[:, 33:34]), "pxs_exp")
            for m in range(8):
                take(("xo", m), lambda h, ps, s: fn(yT[:, m, s], ps, ACT.Copy))
            post(1)
            act.wait_ge(sem("mem_stored"), 32)
            for m in range(32):
                take(("up", m), lambda h, ps, s: fn(hid[:, m, s], ps, ACT.Relu))
            for m in range(4):
                act.wait_ge(sem("down_mm"), 4 * (m + 1))
                for j in range(2):
                    for h in range(2):
                        signal(fn(yT[:, 2 * m + j, h * HALF:(h + 1) * HALF], bank(4 * (m % 2) + 2 * j + h, HALF), ACT.Copy),
                               "down_out")
            post(2)

        @block.vector
        def _(dve):
            own = Own(dve, "dve_steps")
            tt, ts, stt, cp = dve.tensor_tensor, dve.tensor_scalar, dve.scalar_tensor_tensor, dve.tensor_copy

            def link(ins):
                own(ins)
                own.wait()

            def cmul(o, a, b, t, conj=False):
                own.wait()
                own(tt(o[0], a[0], b[0], ALU.mult))
                own(tt(t[0], a[1], b[1], ALU.mult))
                own(tt(o[1], a[0], b[1], ALU.mult))
                own(tt(t[1], a[1], b[0], ALU.mult))
                own.wait()
                own(tt(o[0], o[0], t[0], ALU.add if conj else ALU.subtract))
                own(tt(o[1], o[1], t[1], ALU.subtract if conj else ALU.add))

            def mark(name, *wait):
                own.wait()
                if wait:
                    dve.wait_ge(*wait)
                signal(dve.nop(), name)

            def bc(ap, shape):
                return ap.to_broadcast(shape)

            def prenorm(tag, src, ntiles, dst, j0, tmp, free=None):
                def out(t):
                    n = P if tag == "mem" else tile_rows(t)
                    dve.wait_ge(sem(f"xt_{tag}"), t + 1)
                    g = gain[tag]
                    ins = None
                    for h in range(2):
                        ps = bank(4 + 2 * (t % 2) + h, 4 * P).rearrange("p (k t) -> p k t", k=4)[:, :, 0:n]
                        ins = tt(dst[:, 4 * h:4 * h + 4, tok0(t):tok0(t) + n], ps,
                                 bc(g[:, 4 * h:4 * h + 4].unsqueeze(2), [P, 4, n]), ALU.mult)
                        if h == 0:
                            own(ins)
                    signal(ins, f"xT_{tag}")

                for t in range(ntiles):
                    n = P if tag == "mem" else tile_rows(t)
                    r = slice(j0 + t, j0 + t + 1)
                    dve.wait_ge(sem(f"rms_{tag}"), t + 1)
                    link(dve.reciprocal(rstd[0:n, r], rms[0:n, r]))
                    if t >= 2:
                        out(t - 2)
                    signal(ts(tmp[0:n, t % 2, :], src[0:n, t, :], rstd[0:n, r], None, ALU.mult), f"xn_{tag}")
                for t in range(max(ntiles - 2, 0), ntiles):
                    out(t)

            dve.wait_ge(*step("vecs_T"))
            signal(cp(pv, bank(0, 36)), "gains_ready")
            dve.wait_ge(*step("gains_ready"))
            prenorm("mix", x_a, NT, actT, 0, xn)

            lr = lambda i: lamrow[0:GP, i, :]

            def setup():
                lre, lim = lr(0), lr(1)
                dve.wait_ge(*step("dt_ready"))
                dtb = bc(lamrow[0:GP, 2, 0:2].unsqueeze(2), [GP, 2, 64])
                v3 = lambda i: lamrow[0:GP, i, :].rearrange("g (m s) -> g m s", m=2)
                a, th, k, r = lr(3), lr(4), lr(5), lr(6)
                link(tt(v3(3), v3(0), dtb, ALU.mult))
                link(tt(v3(4), v3(1), dtb, ALU.mult))
                link(ts(k, th, 1.0 / TWO_PI, ROUND, ALU.mult, ALU.add))
                link(ts(k, k, -ROUND, None, ALU.add))
                c1 = 6.28125
                c2 = float(np.float32(TWO_PI - c1) .view(np.uint32) & 0xFFFFF000 and
                           np.array([np.float32(TWO_PI - c1).view(np.uint32) & 0xFFFFF000], np.uint32).view(np.float32)[0])
                c3 = TWO_PI - c1 - c2
                for i, c in enumerate((c1, c2, c3)):
                    link(stt(r, k, -c, th if i == 0 else r, ALU.mult, ALU.add))
                link(ts(lr(8), r, 0.5, math.pi / 2, ALU.mult, ALU.min))
                link(ts(lr(8), lr(8), -math.pi / 2, None, ALU.max))
                link(ts(lr(9), lr(8), -1.0, None, ALU.mult))
                link(tt(lr(9), lr(9), lr(8), ALU.max))
                signal(ts(lr(9), lr(9), -1.0, math.pi / 2, ALU.mult, ALU.add), "half_angles")
                link(ts(a, a, -60.0, 1.0 / 64, ALU.max, ALU.mult))
                m, w = lr(12), lr(13)
                link(ts(m, a, 1.0 / 8, 1.0, ALU.mult, ALU.add))
                for n in (7, 6, 5, 4, 3, 2):
                    link(tt(m, m, a, ALU.mult))
                    link(ts(m, m, 1.0 / n, 1.0, ALU.mult, ALU.add))
                link(tt(m, m, a, ALU.mult))
                for _ in range(6):
                    link(ts(w, m, 2.0, None, ALU.add))
                    link(tt(m, m, w, ALU.mult))
                dve.wait_ge(*step("sines"))
                sh, ch, cm1, sn = lr(10), lr(11), lr(14), lr(15)
                link(tt(cm1, sh, sh, ALU.mult))
                link(tt(sn, sh, ch, ALU.mult))
                link(ts(cm1, cm1, -2.0, None, ALU.mult))
                link(ts(sn, sn, 2.0, None, ALU.mult))
                link(ts(w, m, 1.0, None, ALU.add))
                link(tt(lr(5), m, cm1, ALU.mult))
                link(tt(lr(16), w, sn, ALU.mult))
                link(tt(lr(17), m, cm1, ALU.add))
                link(tt(lr(18), lre, lre, ALU.mult))
                link(tt(lr(19), lim, lim, ALU.mult))
                link(tt(lr(17), lr(17), lr(5), ALU.add))
                link(tt(lr(18), lr(18), lr(19), ALU.add))
                link(dve.reciprocal(lr(18), lr(18)))
                link(tt(lr(5), lr(17), lre, ALU.mult))
                link(tt(lr(6), lr(16), lim, ALU.mult))
                link(tt(lr(7), lr(16), lre, ALU.mult))
                link(tt(lr(8), lr(17), lim, ALU.mult))
                link(tt(lr(5), lr(5), lr(6), ALU.add))
                link(tt(lr(7), lr(7), lr(8), ALU.subtract))
                link(tt(lr(2), lr(5), lr(18), ALU.mult))
                link(tt(lr(3), lr(7), lr(18), ALU.mult))
                link(ts(lr(0), lr(17), 1.0, None, ALU.add))
                link(cp(lr(1), lr(16)))
                link(ts(lr(4), cm1, 1.0, None, ALU.add))
                link(cp(lr(5), sn))
                link(tt(lr(6), w, w, ALU.mult))
                own.wait()
                link(tt(lr(6), lr(6), lr(6), ALU.mult))
                signal(tt(lr(6), lr(6), lr(6), ALU.mult), "lam_ready")
                yield
                dve.wait_ge(*step("lam_T"))
                signal(cp(lam_s.rearrange("p v g -> p (v g)"), bank(7, 7 * GP, 256)), "lam_out")
                dve.wait_ge(*step("c_T"))
                signal(cp(c_in.rearrange("p z g c -> p (z g c)"), bank(7)), "c_out")
                dve.wait_ge(*step("lam_out"))
                dve.wait_ge(*step("c_out"))
                dve.wait_ge(*step("h0_T"))
                for z in range(2):
                    ins = cp(h0raw[:, z * P:(z + 1) * P], bank(7, P, z * P))
                    if z == 0:
                        link(ins)
                signal(ins, "h0_out")
                yield
                link(dve.memset(pw[:, 0, 0, :], 1.0))
                link(dve.memset(pw[:, 1, 0, :], 0.0))
                for z in range(2):
                    link(cp(pw[:, z, 1, :], lam_s[:, z, :]))
                own.wait()
                pt = pwt.rearrange("p (z n g) -> p z n g", z=2, n=4)
                for n in (1, 2, 4):
                    cmul([pw[:, z, n + 1:2 * n + 1, :] for z in range(2)],
                         [bc(pw[:, z, n:n + 1, :], [P, n, GP]) for z in range(2)],
                         [pw[:, z, 1:n + 1, :] for z in range(2)], [pt[:, z, 0:n, :] for z in range(2)])
                    own.wait()
                dve.wait_ge(sem("bc_in"), BC_IN)
                wv = [bc(lam_s[:, 2 + z, :].unsqueeze(2), [P, GP, C_SSM]) for z in range(2)]
                mt = [mtmp[:, z] for z in range(2)]
                cmul([bb[:, z] for z in range(2)], wv, [b_in[:, z] for z in range(2)], mt)
                own.wait()
                pwb = lambda n: [bc(pw[:, z, n, :].unsqueeze(2), [P, GP, C_SSM]) for z in range(2)]
                for j in range(L):
                    cmul([BP[:, z, :, j, :] for z in range(2)], pwb(L - 1 - j), [bb[:, z] for z in range(2)], mt)
                    if j == 3:
                        yield
                own.wait()
                link(dve.memset(cblk.rearrange("p z g m c -> p (z g m c)"), 0.0))
                for m in range(2):
                    s = slice(m * 64, m * 64 + 64)
                    link(cp(cblk[s, 0, :, m, :], c_in[s, 0]))
                    link(ts(cblk[s, 1, :, m, :], c_in[s, 1], -1.0, None, ALU.mult))
                own.wait()
                mark("bp_ready")
                yield
                for i in range(L):
                    cmul([M2[:, z, :, i, :] for z in range(2)], pwb(L - i), [c_in[:, z] for z in range(2)], mt)
                    own.wait()
                    if i % 3 == 2:
                        yield
                link(ts(M2[:, 1].rearrange("p g j c -> p (g j c)"), M2[:, 1].rearrange("p g j c -> p (g j c)"), -1.0, None,
                        ALU.mult))
                while True:
                    yield

            steps = setup()

            def token_tile(m):
                if m < 4:
                    return u_tok[:, :, m * P:(m + 1) * P]
                if m < 8:
                    return q_tok[:, :, (m - 4) * P:(m - 3) * P]
                if m < 14:
                    return kvt[:, :, (m - 8) * P:(m - 7) * P]
                return gtk

            for m in range(15):
                dve.wait_ge(sem("back_T"), m + 1)
                M = 24 if m == 14 else P
                scale = HD ** -0.5 if 4 <= m < 8 else 1.0
                dst = token_tile(m)
                b = 4 + 2 * (m % 2)
                own(ts(dst[0:TS, 4, :], bank(b + 1, M, 0, rows=TS), scale, None, ALU.mult))
                signal(ts(dst[:, 0:4, :], bank(b, 4 * P).rearrange("p (t c) -> p t c", t=4)[:, :, 0:M], scale, None,
                          ALU.mult), "tok_ready")
                if m <= 12:
                    next(steps)

            dve.wait_ge(sem("tok_ready"), 15)

            def rope(t0, t1, rows, tile, heads):
                nt = t1 - t0
                cs = [bc(C(n)[rows].rearrange("p (t f) -> p t f", t=NT)[:, t0:t1, :].unsqueeze(2), [rows.stop, nt, heads, 8])
                      for n in ("cos", "sin")]
                h4 = tile[rows, t0:t1, :].rearrange("p t (h d) -> p t h d", d=HD)
                x1, x2 = h4[:, :, :, 0:8], h4[:, :, :, 8:16]
                tmp = [rope_t[rows, z, 0:nt * heads * 8].rearrange("p (t h f) -> p t h f", t=nt, h=heads) for z in range(2)]
                own(tt(tmp[0], x2, cs[1], ALU.mult))
                own(tt(tmp[1], x1, cs[1], ALU.mult))
                own.wait()
                own(tt(x1, x1, cs[0], ALU.mult))
                own(tt(x2, x2, cs[0], ALU.mult))
                own.wait()
                own(tt(x1, x1, tmp[0], ALU.subtract))
                return tt(x2, x2, tmp[1], ALU.add)

            for kind in (0, 2, 4):
                for t0, t1, rows in ((0, 4, slice(0, P)), (4, 5, slice(0, TS))):
                    ins = rope(t0, t1, rows, kvt[:, :, kind * P:(kind + 1) * P], 2)
                    if (kind, t0) != (4, 4):
                        own(ins)
                        own.wait()
            signal(ins, "roped")
            for t0, t1, rows in ((0, 4, slice(0, P)), (4, 5, slice(0, TS))):
                dve.wait_ge(*step("roped"))
                ins = rope(t0, t1, rows, q_tok, NH)
                if t0 == 0:
                    link(ins)
            signal(ins, "q_roped")

            dve.wait_ge(sem("gk_out"), 16)
            for n in range(8):
                dve.wait_ge(sem("m1_T"), n + 1)
                z, g = n // 4, n % 4 * 4
                signal(cp(M1[:, z, g:g + 4, :].rearrange("p g s -> p (g s)"), bank(4 + n % 2)), "m1_out")
            own(tt(dterm.rearrange("p (g c) -> p g c", c=C_SSM), drow.rearrange("p (g c) -> p g c", c=C_SSM),
                   bc(C("dmask").unsqueeze(1), [P, G_SSM, C_SSM]), ALU.mult))
            own.wait()
            dve.wait_ge(*step("lags_mm"))
            signal(tt(G, bank(6), dterm, ALU.add), "lags_ready")
            for i in range(6):
                dve.wait_ge(sem("qk_T"), i + 1)
                dst = qT[:, i, 0:TP] if i < 4 else kT[:, i - 4, 0:TP]
                signal(cp(dst, bank(4 + i % 2)), "qk_out")
            own(cp(qT[:, :, TP:TOK], bank(7, 4 * TS).rearrange("p (r t) -> p r t", r=4)))
            signal(cp(kT[:, :, TP:TOK], bank(7, 2 * TS, 4 * TS).rearrange("p (b t) -> p b t", b=2)), "qk_out")
            mark("q_read")

            uu = [u8[:, z * GP:(z + 1) * GP] for z in range(2)]
            cc = [[cur[:, (s * 2 + z) * GP:(s * 2 + z + 1) * GP] for z in range(2)] for s in range(2)]
            pt = [pwt[:, z * GP:(z + 1) * GP] for z in range(2)]
            base = [lam_s[:, 4 + z, :] for z in range(2)]
            cmul(cc[0], base, base, pt)
            own.wait()
            cmul(cc[1], cc[0], cc[0], pt)
            own.wait()
            cmul(cc[0], cc[1], cc[1], pt)
            own.wait()
            own(dve.memset(E[:, 0, :, 0:1], 1.0))
            own(dve.memset(E[:, 1, :, 0:1], 0.0))
            own.wait()
            n, s = 1, 0
            while n < NCH:
                cmul([E[:, z, :, n:2 * n] for z in range(2)], [bc(cc[s][z].unsqueeze(2), [P, GP, n]) for z in range(2)],
                     [E[:, z, :, 0:n] for z in range(2)], [rt[:, :, 0:n], rt[:, :, 32:32 + n]])
                own.wait()
                cmul(cc[1 - s], cc[s], cc[s], pt)
                own.wait()
                n, s = 2 * n, 1 - s
            own(cp(rho, bc(lam_s[:, 6, :].unsqueeze(2), [P, GP, NCH])))
            own.wait()
            link(dve.memset(rho[:, :, 0:1], 0.0))

            dve.wait_ge(sem("gk_out"), 32)
            for n in range(6):
                dve.wait_ge(sem("ut_T"), n + 1)
                k = min(6, G_SSM - n * 6)
                signal(cp(UT[:, n * 6:n * 6 + k, :].rearrange("p g n -> p (g n)"), bank(6 + n % 2, k * UROWS)), "ut_out")
            dve.wait_ge(*step("z_mm"))
            for z in range(2):
                for b in range(3):
                    k = min(6, GP - b * 6)
                    own(cp(Z[:, z, b * 6:b * 6 + k, :].rearrange("p g n -> p (g n)"), bank(z * 3 + b, k * UROWS)))
            own.wait()
            mark("z_out")
            En = [E[:, z] for z in range(2)]
            cmul([W[:, z] for z in range(2)], En, [Z[:, z, :, 0:NCH] for z in range(2)], [rt, Gs[:, 0]], conj=True)
            own.wait()
            for z in range(2):
                own(dve.tensor_tensor_scan(Gs[:, z].rearrange("p g n -> p (g n)"), rho.rearrange("p g n -> p (g n)"),
                                           W[:, z].rearrange("p g n -> p (g n)"), 0.0, ALU.mult, ALU.add))
            own.wait()
            last = NCH - 1
            cmul([hfp[:, z] for z in range(2)], [E[:, z, :, last] for z in range(2)], [Gs[:, z, :, last] for z in range(2)], pt)
            cmul([Z[:, z, :, 1:NCH] for z in range(2)], [E[:, z, :, 0:last] for z in range(2)],
                 [Gs[:, z, :, 0:last] for z in range(2)], [W[:, z, :, 0:last] for z in range(2)])
            own.wait()
            h0v = [h0raw[:, z * P:(z + 1) * P].rearrange("p (b g) -> p b g", b=DB) for z in range(2)]
            for z in range(2):
                own(dve.memset(Z[:, z, :, 0:1], 0.0))
                own(cp(Z[:, z, :, NCH:YROWS].rearrange("p g b -> p b g"), h0v[z]))
            own.wait()
            mark("h_ready")
            cmul([hfs[:, z] for z in range(2)], [bc(pw[:, z, 4:5, :], [P, DB, GP]) for z in range(2)], h0v,
                 [rt[:, z * 8:z * 8 + 2, :].rearrange("p a n -> p (a n)").rearrange("p (b g) -> p b g", b=DB) for z in range(2)])
            own.wait()
            for z in range(2):
                own(tt(hfs[:, z], hfs[:, z], Z[:, z, :, YROWS:UROWS].rearrange("p g b -> p b g"), ALU.add))
            own.wait()
            mark("hfin_ready")
            for n in range(8):
                dve.wait_ge(sem("y_mm"), n + 1)
                src = bank(6 + n % 2, 4 * P, rows=YROWS).rearrange("p (g i c) -> p g i c", g=4, i=L)
                dst = y_sb[0:YROWS, :, n // 2 * 128:n // 2 * 128 + 128].rearrange("p i (g m c) -> p g m i c", g=4, m=2)[:, :, n % 2]
                signal(cp(dst, src), "y_out")
            dve.wait_ge(*step("hfin_T"))
            own(cp(hout[0:GP, 0:256].rearrange("g (s z) -> g z s", z=2), bank(4, 256, rows=GP).rearrange("g (z s) -> g z s", z=2)))
            signal(cp(hout[:, 256:512].rearrange("g (s z) -> g z s", z=2), bank(4, 256, 256).rearrange("g (z s) -> g z s", z=2)),
                   "ssm_states")
            for m in range(4):
                dve.wait_ge(sem("lin_out"), 2 * (unit[("glu", m)] + 1))
                ins = tt(ssmT[:, m, :], yg[:, m, :], sg[:, m, :], ALU.mult)
                if m < 3:
                    own(ins)
            signal(ins, "ssm_read")

            def prompt_rows(v):
                if v == 0:
                    dve.wait_ge(sem("y_mm"), 8)
                else:
                    dve.wait_ge(sem("cmp_done"), 2)
                signal(cp(ck[3 * v][:, NP0:NP0 + 4, :], kvt[:, 0:4, v * P:(v + 1) * P]), "prompt_rows")

            def cmp_take(cu):
                dve.wait_ge(sem("cmp2_mm"), cu + 1)
                (v, s0, ns), first = cmp_units[cu], cu % 3 == 0
                if v == 0:
                    if first:
                        own(cp(kcT[:, 256:264], bank(6, 8, P + 2 * NP0)))
                    signal(cp(kcT[:, s0 * 32:(s0 + ns) * 32], bank(6, ns * 32, P)), "cmp_out")
                else:
                    if first:
                        own(cp(vcp[0:8, :], bank(6, P, P + ns * P, rows=8)))
                    signal(cp(vc[0:32, s0:s0 + ns, :].rearrange("p b c -> p (b c)"), bank(6, ns * P, P, rows=32)), "cmp_out")

            prompt_rows(0)

            gate_v = gtk.rearrange("p t (g r j) -> p t r g j", g=2, r=REP)

            def take_o(idx, ps_bank):
                if idx < 8:
                    br, qt = idx // 4, idx % 4
                    if idx:
                        dve.wait_ge(sem("o_taken"), idx)
                    sc = pscale[:, idx % 2 * 8:idx % 2 * 8 + 8]
                    link(dve.reciprocal(sc, rsum[:, idx * 8:idx * 8 + 8]))
                    sc2 = sc.rearrange("p (r g) -> p r g", g=2)
                    link(tt(sc2, sc2, gate_v[:, qt, :, :, br + 1], ALU.mult))
                    ps = bank(ps_bank).rearrange("p (h d) -> p h d", h=8)
                    scb = bc(sc.unsqueeze(2), [P, 8, 64])
                    if br == 0:
                        signal(tt(o_acc[:, qt, :].rearrange("p (h d) -> p h d", h=8), ps, scb, ALU.mult), "o_taken")
                        return
                    link(tt(ps, ps, scb, ALU.mult))
                    signal(tt(o_acc[:, qt, :], o_acc[:, qt, :], bank(ps_bank), ALU.add), "o_taken")

            for i in range(64 + 3):
                if i < 64:
                    qt = i // 8 % 4
                    dve.wait_ge(sem("s_done"), i + 1)
                    diag = bank(S_BANKS[i % 3], P, qt * P)
                    link(tt(diag, diag, C("causal"), ALU.add))
                    signal(dve.tensor_reduce(nmx[:, i:i + 1], bank(S_BANKS[i % 3], (qt + 1) * P), AX.X, ALU.max, negate=True), "mx_done")
                if 2 <= i < 66:
                    j = i - 2
                    qt = j // 8 % 4
                    dve.wait_ge(sem("p_T"), j + 1)
                    if j >= 2:
                        dve.wait_ge(sem("pv_done"), j - 1)
                    signal(cp(pT[:, j % 2, 0:(qt + 1) * P], bank(2 + j % 2, (qt + 1) * P)), "pT_ready")
                if i >= 3 and (i - 3) % 8 == 7:
                    idx = (i - 3) // 8
                    dve.wait_ge(sem("pv_done"), 8 * idx + 8)
                    take_o(idx, 4 + idx % 2)
                if i in CMP2_AT:
                    cmp_take(CMP2_AT.index(i))
                    if i == CMP2_AT[1]:
                        prompt_rows(1)
            dve.wait_ge(*step("sc_done"))
            S3 = lambda ap: ap.rearrange("p (h n) -> p h n", n=8)
            S4 = lambda ap: ap.rearrange("p (q h n) -> p q h n", q=4, n=8)
            cmask = lambda n, h=8: bc(C(n).rearrange("p (q n) -> p q n", q=4).unsqueeze(2), [P, 4, h, 8])
            for g in range(2):
                link(tt(pc_s.rearrange("p (q r g n) -> p q r g n", q=4, r=REP, g=2)[:, :, :, g, :],
                        bank(g, 128).rearrange("p (q r n) -> p q r n", q=4, r=REP), cmask("cadd", REP), ALU.add))
            link(dve.tensor_reduce(pscale[:, 16:48], S3(pc_s), AX.X, ALU.max))
            signal(tt(S3(pc_s), S3(pc_s), bc(pscale[:, 16:48].unsqueeze(2), [P, 32, 8]), ALU.subtract), "pc_shifted")
            dve.wait_ge(*step("pc_exp"))
            link(tt(S4(pc_e), S4(pc_e), cmask("cmul"), ALU.mult))
            link(dve.tensor_reduce(pscale[:, 16:48], S3(pc_e), AX.X, ALU.add))
            link(ts(pscale[:, 16:48], pscale[:, 16:48], 1e-30, None, ALU.max))
            link(dve.reciprocal(pscale[:, 16:48], pscale[:, 16:48]))
            for qt in range(4):
                p4 = pscale[:, 16 + 8 * qt:24 + 8 * qt].rearrange("p (r g) -> p r g", g=2)
                own(tt(p4, p4, gate_v[:, qt, :, :, 0], ALU.mult))
            own.wait()
            signal(tt(S3(pc_s), S3(pc_e), bc(pscale[:, 16:48].unsqueeze(2), [P, 32, 8]), ALU.mult), "pc_ready")
            for n in range(8):
                dve.wait_ge(sem("pc_T"), n + 1)
                signal(cp(pcT[0:8, n * 4:n * 4 + 4, :].rearrange("p h q -> p (h q)"), bank(2 + n % 2, rows=8)), "pcT_out")
            dve.wait_ge(sem("o_taken"), 8)
            for qt in range(4):
                dve.wait_ge(sem("pv_done"), 65 + qt)
                signal(tt(o_acc[:, qt, :], bank(4 + qt % 2), o_acc[:, qt, :], ALU.add), "o_taken")
            for qt in range(4):
                dve.wait_ge(sem("o_T"), qt + 1)
                signal(cp(nsaT[:, :, qt * P:(qt + 1) * P], bank(6 + qt % 2).rearrange("p (r t) -> p r t", r=REP)), "nsa_out")
            dve.wait_ge(sem("o_taken"), 12)
            mark("prompt_attn_done")

            dve.wait_ge(*step("qbd_zeroed"))
            for g in range(2):
                s = slice(g * 64, g * 64 + 64)
                for r in range(REP):
                    own(cp(qbd[s].rearrange("p b (g q r) -> p b g q r", g=2, q=DQ)[:, :, g, :, r],
                           qT[s, r, TP:TOK].rearrange("p (b q) -> p b q", q=DQ)))
            own.wait()
            mark("qbd_ready")
            for gg in range(NG2):
                dve.wait_ge(sem("gs_mm"), gg + 1)
                link(tt(gtmp.rearrange("p (h j) -> p h j", j=3), bank(6, 24).rearrange("p (h j) -> p h j", j=3),
                        bc(C("hmask").unsqueeze(2), [P, NH, 3]), ALU.mult))
                link(dve.tensor_reduce(gs[:, gg, :], gtmp.rearrange("p (h j) -> p j h", j=3), AX.X, ALU.add))
                dve.wait_ge(sem("sc_s_mm"), gg + 1)
                signal(dve.tensor_reduce(sst[:, 0:1], bank(7, 32), AX.X, ALU.max, negate=True), "pcs_max")
                dve.wait_ge(sem("pcs_exp"), gg + 1)
                link(dve.reciprocal(sst[:, 1:2], sst[:, 1:2]))
                signal(ts(pcs, pcs, sst[:, 1:2], None, ALU.mult), "pc_s_ready")
                dve.wait_ge(sem("imp_mm"), gg + 1)
                link(cp(imp, bank(6, 32, 64)))
                nc_ = NBLK - 2
                bi = bc(imp[:, 1:31].unsqueeze(1), [P, nc_, nc_])
                bj = bc(imp[:, 1:31].unsqueeze(2), [P, nc_, nc_])
                k1, k2 = (r_.rearrange("p (j i) -> p j i", j=nc_) for r_ in (rk, rk2))
                own(tt(k1, bi, bj, ALU.is_gt))
                link(tt(k2, bi, bj, ALU.is_equal))
                link(tt(rk2, rk2, C("before"), ALU.mult))
                link(tt(rk, rk, rk2, ALU.add))
                own(dve.memset(selm, 0.0))
                link(dve.tensor_reduce(selm2, k1, AX.X, ALU.add))
                link(ts(selm[:, 1:31], selm2, NSEL - 3 - 0.5, NEG, ALU.is_gt, ALU.mult))
                dve.wait_ge(sem("pc_s_ready"), gg + 1)
                signal(ts(pcs, pcs, gs[:, gg, 0:1], None, ALU.mult), "pcg_ready")
                for kc in range(5):
                    dve.wait_ge(sem("s_mm"), gg * 20 + kc * 4 + 4)
                    ps = bank(2 + (gg * 5 + kc) % 2)
                    if kc < 4:
                        signal(tt(s_sel[:, kc * 512:(kc + 1) * 512].rearrange("p (n k) -> p n k", k=BLK),
                                  ps.rearrange("p (n k) -> p n k", k=BLK),
                                  bc(selm[:, kc * 8:kc * 8 + 8].unsqueeze(2), [P, 8, BLK]), ALU.add), "s_out")
                    else:
                        own(tt(s_win[:, 0:DQ], ps[:, 0:DQ], C("winadd"), ALU.add))
                        signal(cp(s_win[:, DQ:WIN], ps[:, DQ:WIN]), "s_out")
                dve.wait_ge(sem("snew_mm"), gg + 1)
                na = C("newadd")[:, gg * TS:(gg + 1) * TS]
                own(tt(s_sel[:, PAST:PAST + TS], bank(6, TS, 128), na, ALU.add))
                own(tt(s_win[:, WIN:WIN + TS], bank(6, TS, 160), na, ALU.add))
                dve.wait_ge(sem("s_out"), gg * 5 + 5)
                own.wait()
                own(dve.tensor_reduce(sst[:, 2:3], s_sel, AX.X, ALU.max, negate=True))
                signal(dve.tensor_reduce(sst[:, 4:5], s_win, AX.X, ALU.max, negate=True), "sel_max")
                for i, (tile, name) in enumerate(((s_sel, "p_sel"), (s_win, "p_win"))):
                    c = sst[:, 3 + 2 * i:4 + 2 * i]
                    dve.wait_ge(sem("sel_exp"), 2 * gg + i + 1)
                    link(dve.reciprocal(c, c))
                    link(tt(c, c, gs[:, gg, i + 1:i + 2], ALU.mult))
                    signal(ts(tile, tile, c, None, ALU.mult), name)
                dve.wait_ge(sem("pcs_T"), gg + 1)
                if gg:
                    dve.wait_ge(sem("sample_pv"), 4 * gg)
                signal(cp(pcT_s[0:32, :], bank(7, P, 64, rows=32)), "pcs_out")
                for n in range(6):
                    dve.wait_ge(sem("ps_T"), gg * 6 + n + 1)
                    b_ = 4 + (gg * 6 + n) % 2
                    if n < 4:
                        signal(cp(pT_sel[:, n * 4:n * 4 + 4, :].rearrange("p n q -> p (n q)"), bank(b_)), "ps_out")
                    elif n == 4:
                        own(cp(pT_sel[0:TS, 16, :], bank(b_, P, 0, rows=TS)))
                        signal(cp(pT_win[0:TS, 4, :], bank(b_, P, P, rows=TS)), "ps_out")
                    else:
                        signal(cp(pT_win[:, 0:4, :].rearrange("p n q -> p (n q)"), bank(b_)), "ps_out")
                dve.wait_ge(sem("sample_pv"), 4 * (gg + 1))
                signal(cp(so_sb, bank(7, P, 256)), "so_out")
                dve.wait_ge(sem("so_T"), gg + 1)
                for g in range(2):
                    s = slice(g * 64, g * 64 + 64)
                    src = psum[s, 7, 384:512].rearrange("p (b g q r) -> p g r b q", b=4, g=2, q=DQ)[:, g]
                    dst = nsaT[s, :, TP + gg * 16:TP + gg * 16 + 16].rearrange("p r (b q) -> p r b q", q=DQ)
                    ins = cp(dst, src)
                    if g == 0:
                        own(ins)
                signal(ins, "nsa_s_out")

            for m in range(KD):
                dve.wait_ge(sem("lin_out"), 2 * (unit[("bn", m)] + 1))
                own(tt(brt[:, 0, :], brt[:, 0, :], g0[:, m, :], ALU.mult))
                own(tt(brt[:, 1, :], brt[:, 1, :], g1[:, m, :], ALU.mult))
                own.wait()
                signal(tt(mrg[:, m, :], brt[:, 0, :], brt[:, 1, :], ALU.add), "merged")

            def post(i):
                dve.wait_ge(sem("gb_in"), 16 * (i + 1))
                if i == 0:
                    dve.wait_ge(sem("x2_in"), 80)
                for t in range(NT):
                    n = tile_rows(t)
                    dve.wait_ge(sem("rms_post"), i * NT + t + 1)
                    link(dve.reciprocal(rstd[0:n, t:t + 1], rms[0:n, t:t + 1]))
                    ps = psum[0:n, 4 + 2 * (t % 2):6 + 2 * (t % 2), :].rearrange("p b c -> p (b c)")
                    if i * NT + t:
                        dve.wait_ge(sem("post_added"), i * NT + t)
                    link(stt(ptmp[0:n, :], ps, rstd[0:n, t:t + 1], gb[0:n, :], ALU.mult, ALU.mult))
                    signal(tt(x[0:n, t, :], x[0:n, t, :], ptmp[0:n, :], ALU.add), "post_added")
                    if i == 2:
                        mark("y_ready", sem("post_added"), i * NT + t + 1)
                dve.wait_ge(sem("post_added"), (i + 1) * NT)
                mark("post_norms")

            prenorm("mem", memx, 2, mnT, 5, nrm)
            for i in range(8):
                kind, c, t = i // 4, i // 2 % 2, i % 2
                dve.wait_ge(sem("mem_mm"), i + 1)
                signal(cp((kx, vx)[kind][:, t, c * 256:(c + 1) * 256], bank(4 + i % 2, 256)), "mem_out")
            mark("mem_done", sem("mem_out"), 8)
            dve.wait_ge(*step("kx_T"))
            for b in range(2):
                signal(cp(kxT[:, 2 * b:2 * b + 2, :].rearrange("p h m -> p (h m)"), bank(6 + b)), "kxT_out")
            post(0)
            dve.wait_ge(sem("post_norms"), 1)
            prenorm("x", x, NT, actT, 8, nrm)
            mark("x_c_ready", sem("xT_x"), NT)
            for i in range(6):
                if i < 4:
                    dve.wait_ge(sem("sx_done"), i + 1)
                    signal(dve.tensor_reduce(xst[:, i * 8:i * 8 + 4],
                                             psum[:, 0:2, :].rearrange("p b (h m) -> p (b h) m", h=2), AX.X, ALU.max, negate=True),
                           "mxx_done")
                if 1 <= i <= 4:
                    j = i - 1
                    dve.wait_ge(sem("px_T"), j + 1)
                    for b in range(2):
                        signal(cp(pxT[:, j % 2, 2 * b:2 * b + 2].rearrange("p h m q -> p (h m q)"), bank(2 + b)), "pxT_out")
                    dve.wait_ge(sem("ox_mm"), j + 1)
                    link(dve.reciprocal(xst[:, j * 8 + 4:j * 8 + 8], xst[:, j * 8 + 4:j * 8 + 8]))
                    if j >= 2:
                        dve.wait_ge(sem("ox_T"), j - 1)
                    signal(tt(ox[:, j % 2, :].rearrange("p (h d) -> p h d", h=XH), bank(4 + j % 2).rearrange("p (h d) -> p h d", h=XH),
                              bc(xst[:, j * 8 + 4:j * 8 + 8].unsqueeze(2), [P, XH, XD]), ALU.mult), "ox_norm")
                if i >= 2:
                    j = i - 2
                    dve.wait_ge(sem("ox_T"), j + 1)
                    signal(cp(oxT[:, :, j * P:(j + 1) * P], bank(6).rearrange("p (h t) -> p h t", h=XH)), "oxT_out")
            dve.wait_ge(*step("qz_zeroed"))
            for b in range(DB):
                for h in range(XH):
                    c0 = (b % 2) * 16 + h * DQ
                    ins = cp(qz[:, b, h, c0:c0 + DQ], qxT[:, h, TP + b * DQ:TP + (b + 1) * DQ])
                    if (b, h) != (DB - 1, XH - 1):
                        own(ins)
            signal(ins, "qz_ready")
            for b in range(DB):
                dve.wait_ge(sem("kxs_T"), b + 1)
                if b >= 1:
                    dve.wait_ge(sem("kxs_mm"), b)
                for j in range(2):
                    signal(cp(kxsT[:, 2 * j:2 * j + 2, :].rearrange("p h m -> p (h m)"), bank(j)), "kxsT_out")
            dve.wait_ge(sem("kxs_mm"), DB)
            signal(dve.tensor_reduce(xst[:, 32:33], bank(7, 256), AX.X, ALU.max, negate=True), "mxs_done")
            dve.wait_ge(*step("pxs_exp"))
            link(dve.reciprocal(xst[:, 33:34], xst[:, 33:34]))
            signal(ts(pxs, pxs, xst[:, 33:34], None, ALU.mult), "pxs_ready")
            dve.wait_ge(*step("pxs_T"))
            signal(cp(pxsT.rearrange("p m q -> p (m q)"), bank(7, 256, 256)), "pxsT_out")
            dve.wait_ge(sem("xs_used"), DB)
            signal(cp(oxT[:, :, TP:TOK], bank(6, XH * TS).rearrange("p (h t) -> p h t", h=XH)), "oxs_out")
            post(1)
            dve.wait_ge(sem("post_norms"), 2)
            prenorm("mlp", x, NT, actT, 8, nrm)
            for m in range(32):
                for h in range(2):
                    dve.wait_ge(sem("lin_out"), 2 * unit[("up", m)] + h + 1)
                    s = hid[:, m, h * HALF:(h + 1) * HALF]
                    signal(tt(s, s, s, ALU.mult), "hid_ready")
            post(2)


_INS = ["x_prompt", "x_sample", "cache_nsa_kv", "cache_win_kv", "state_ssm", "cache_mem_kv", "page_table", "mem_prompt",
        "g_mix_pre", "w_in", "ssm_lam_re", "ssm_lam_im", "ssm_log_dt", "ssm_b_re", "ssm_b_im", "ssm_c_re", "ssm_c_im",
        "ssm_d", "w_glu", "b_glu", "cmp_pe_k", "w_cmpk1", "w_cmpk2", "cmp_pe_v", "w_cmpv1", "w_cmpv2", "w_br_ssm",
        "w_br_nsa", "w_out", "g_mix_post", "g_x_pre", "g_mem", "w_xq", "w_xk", "w_xv", "w_xo", "g_x_post", "g_mlp_pre",
        "w_up", "w_down", "g_mlp_post"]
_OUTS = [(1, TP, D), (DB, DQ, D), (1, 1, TP, 4, NKV, HD), (1, DB, DQ, 4, NKV, HD), (1, 1, WIN, 2, NKV, HD),
         (1, DB, WIN, 2, NKV, HD), (1, 1, G_SSM, S_SSM, 2), (1, DB, G_SSM, S_SSM, 2), (1, 1, MEM, 2, XH, XD)]


def kernel(**inputs):
    import concourse.bacc as _bacc
    from concourse.bass_utils import run_bass_kernel_spmd as _run

    nc = _bacc.Bacc("TRN2", target_bir_lowering=False, num_devices=1)
    arrays, A = {}, {}
    for name in _INS + ["consts"]:
        a = np.ascontiguousarray(constants() if name == "consts" else inputs[name])
        arrays[f"in_{name}"] = a
        A[name] = nc.dram_tensor(f"in_{name}", a.shape, mybir.dt.from_np(a.dtype), kind="ExternalInput").ap()
    O = [nc.dram_tensor(f"out_{i}", s, F32, kind="ExternalOutput").ap() for i, s in enumerate(_OUTS)]
    hybrid_decoder_layer(nc, A, O)
    r = _run(nc, [arrays], core_ids=[0])
    return tuple(r.results[0][f"out_{i}"] for i in range(len(_OUTS)))
```
